# Optimizing a Trainium2 kernel written in Bass

```python
import jax, jax.numpy as jnp
from jax import lax
import numpy as np

D_MODEL = 1024
BATCH = 1
SEQ = 1024
DEPTH = 2
DEC_BATCH = 8
DEC_SEQ = 8
PAST_LEN = 1024
PAGE_SIZE = 128

HEAD_DIM = 64
A_HEADS = 16
A_KV_HEADS = 4
A_GROUP = A_HEADS // A_KV_HEADS
A_WINDOW = 128
A_Q_W = A_HEADS * HEAD_DIM
A_KV_W = A_KV_HEADS * HEAD_DIM
A_QKV_WIDTH = A_Q_W + 2 * A_KV_W
B_SLOTS = 8
B_PATTERNS = ((128, 1), (512, 4), (2048, 16))
B_N_GROUPS = len(B_PATTERNS)
B_HEADS = B_N_GROUPS * B_SLOTS
B_MAX_WINDOW = max(w for w, _ in B_PATTERNS)
D_FF = -(-8 * D_MODEL // (3 * 256)) * 256
N_A_LAYERS = DEPTH // 2
N_B_LAYERS = DEPTH - N_A_LAYERS
BLOCK = 128
EPS = 1e-6
NEG = -1e30

kernel_name = 'yoco_swa_sink_dilated_decode_step'

def rms_norm(x, g):
    xf = x.astype(jnp.float32)
    y = xf * lax.rsqrt(jnp.mean(xf * xf, axis=-1, keepdims=True) + EPS)
    return y.astype(x.dtype) * g

def alibi_slopes(n):
    return jnp.asarray(2.0 ** (-8.0 * (np.arange(n) + 1) / n), dtype=jnp.float32)

def swiglu(x, w_gu, w_dn):
    gate, up = jnp.split(x @ w_gu, 2, axis=-1)
    return (jax.nn.silu(gate) * up) @ w_dn

def qkv_a(h, w_qkv):
    n, t = h.shape[:2]
    q, k, v = jnp.split(h @ w_qkv, [A_Q_W, A_Q_W + A_KV_W], axis=-1)
    return (q.reshape(n, t, A_KV_HEADS, A_GROUP, HEAD_DIM),
            k.reshape(n, t, A_KV_HEADS, HEAD_DIM),
            v.reshape(n, t, A_KV_HEADS, HEAD_DIM))

def shared_kv(x, g_kv, w_kv_s):
    n, t = x.shape[:2]
    k, v = jnp.split(rms_norm(x, g_kv) @ w_kv_s, 2, axis=-1)
    return k.reshape(n, t, B_SLOTS, HEAD_DIM), v.reshape(n, t, B_SLOTS, HEAD_DIM)

def banded_attention(q, k, v, slopes, dist_unit, max_dist, sinks=None):
    n, L, kh, g, d = q.shape
    nb = -(-L // BLOCK)
    pad = nb * BLOCK - L
    q = jnp.pad(q, ((0, 0), (0, pad), (0, 0), (0, 0), (0, 0)))
    k = jnp.pad(k, ((0, 0), (BLOCK, pad), (0, 0), (0, 0)))
    v = jnp.pad(v, ((0, 0), (BLOCK, pad), (0, 0), (0, 0)))
    qb = q.reshape(n, nb, BLOCK, kh, g, d)
    kb = k.reshape(n, nb + 1, BLOCK, kh, d)
    vb = v.reshape(n, nb + 1, BLOCK, kh, d)
    kc = jnp.concatenate([kb[:, :-1], kb[:, 1:]], axis=2)
    vc = jnp.concatenate([vb[:, :-1], vb[:, 1:]], axis=2)
    s = jnp.einsum('nbqhgd,nbkhd->nbhgqk', qb, kc).astype(jnp.float32) * HEAD_DIM ** -0.5
    qi = jnp.arange(BLOCK)[:, None]
    kj = jnp.arange(2 * BLOCK)[None, :]
    dist = BLOCK + qi - kj
    kpos = jnp.arange(nb)[:, None, None] * BLOCK + kj[None] - BLOCK
    valid = (dist >= 0) & (dist <= max_dist) & (kpos >= 0)
    s = s - slopes[None, None, :, :, None, None] * (dist_unit * dist).astype(jnp.float32)
    s = jnp.where(valid[None, :, None, None], s, NEG)
    lse = jax.nn.logsumexp(s, axis=-1)
    if sinks is not None:
        lse = jnp.logaddexp(lse, sinks.astype(jnp.float32)[None, None, :, :, None])
    p = jnp.exp(s - lse[..., None])
    o = jnp.einsum('nbhgqk,nbkhd->nbqhgd', p.astype(v.dtype), vc)
    o = o.reshape(n, nb * BLOCK, kh, g, d)[:, :L]
    lse = jnp.moveaxis(lse, -1, 2).reshape(n, nb * BLOCK, kh, g)[:, :L]
    return o, lse

def window_attention_sample(q, kc, vc, slopes, sinks):
    S = q.shape[1]
    W = kc.shape[1] - S
    s = jnp.einsum('bqhgd,bkhd->bhgqk', q, kc).astype(jnp.float32) * HEAD_DIM ** -0.5
    dist = (W + jnp.arange(S))[:, None] - jnp.arange(W + S)[None, :]
    valid = (dist >= 0) & (dist < A_WINDOW)
    s = s - slopes[None, :, :, None, None] * dist.astype(jnp.float32)
    s = jnp.where(valid, s, NEG)
    lse = jnp.logaddexp(jax.nn.logsumexp(s, axis=-1), sinks.astype(jnp.float32)[None, :, :, None])
    p = jnp.exp(s - lse[..., None])
    return jnp.einsum('bhgqk,bkhd->bqhgd', p.astype(vc.dtype), vc)

def to_sub(x, r):
    n, t = x.shape[:2]
    rest = x.shape[2:]
    x = jnp.swapaxes(x.reshape((n, t // r, r) + rest), 1, 2)
    return x.reshape((n * r, t // r) + rest)

def from_sub(x, n, r):
    L = x.shape[1]
    rest = x.shape[2:]
    x = jnp.swapaxes(x.reshape((n, r, L) + rest), 1, 2)
    return x.reshape((n, L * r) + rest)

def combine_groups(outs, lses):
    wts = jax.nn.softmax(jnp.stack(lses, axis=0), axis=0)
    return jnp.einsum('gnts,gntsd->ntsd', wts.astype(outs[0].dtype), jnp.stack(outs, axis=0))

def dilated_prompt(q, k, v, slopes):
    n = q.shape[0]
    outs, lses = [], []
    for gi, (w, r) in enumerate(B_PATTERNS):
        qs = to_sub(q[:, :, gi], r)[:, :, :, None]
        o, lse = banded_attention(qs, to_sub(k, r), to_sub(v, r), slopes[gi][:, None], r, w // r)
        outs.append(from_sub(o[:, :, :, 0], n, r))
        lses.append(from_sub(lse[..., 0], n, r))
    return combine_groups(outs, lses)

def dilated_sample(q, kc, vc, slopes):
    S = q.shape[1]
    W = kc.shape[1] - S
    outs, lses = [], []
    for gi, (w, r) in enumerate(B_PATTERNS):
        steps = jnp.arange(w // r + 1)
        idx = W + jnp.arange(S)[:, None] - r * steps[None, :]
        valid = idx >= 0
        idx = jnp.maximum(idx, 0)
        kg = kc[:, idx]
        vg = vc[:, idx]
        s = jnp.einsum('bshd,bskhd->bhsk', q[:, :, gi], kg).astype(jnp.float32) * HEAD_DIM ** -0.5
        s = s - slopes[gi][None, :, None, None] * (r * steps).astype(jnp.float32)
        s = jnp.where(valid[None, None], s, NEG)
        lse = jax.nn.logsumexp(s, axis=-1)
        p = jnp.exp(s - lse[..., None])
        outs.append(jnp.einsum('bhsk,bskhd->bshd', p.astype(vc.dtype), vg))
        lses.append(jnp.swapaxes(lse, 1, 2))
    return combine_groups(outs, lses)

def setup_inputs(seed: int = 0) -> dict:
    key = jax.random.key(seed)
    ks = jax.random.split(key, 18)
    wa = min(A_WINDOW, PAST_LEN)
    wb = min(B_MAX_WINDOW, PAST_LEN)

    def nrm(k, shape, scale=1.0):
        return scale * jax.random.normal(k, shape, jnp.float32)

    return {
        'x_prompt': nrm(ks[0], (BATCH, SEQ, D_MODEL)),
        'x_sample': nrm(ks[1], (DEC_BATCH, DEC_SEQ, D_MODEL)),
        'cache_a_k': nrm(ks[2], (N_A_LAYERS, DEC_BATCH, wa, A_KV_HEADS, HEAD_DIM)),
        'cache_a_v': nrm(ks[3], (N_A_LAYERS, DEC_BATCH, wa, A_KV_HEADS, HEAD_DIM)),
        'cache_b_k': nrm(ks[4], (DEC_BATCH, wb, B_SLOTS, HEAD_DIM)),
        'cache_b_v': nrm(ks[5], (DEC_BATCH, wb, B_SLOTS, HEAD_DIM)),
        'g_attn': 1.0 + nrm(ks[6], (DEPTH, D_MODEL), 0.05),
        'g_ffn': 1.0 + nrm(ks[7], (DEPTH, D_MODEL), 0.05),
        'w_qkv_a': nrm(ks[8], (N_A_LAYERS, D_MODEL, A_QKV_WIDTH), D_MODEL ** -0.5),
        'sinks_a': nrm(ks[9], (N_A_LAYERS, A_HEADS), 0.5),
        'w_o_a': nrm(ks[10], (N_A_LAYERS, A_Q_W, D_MODEL), A_Q_W ** -0.5),
        'g_kv': 1.0 + nrm(ks[11], (D_MODEL,), 0.05),
        'w_kv_s': nrm(ks[12], (D_MODEL, 2 * B_SLOTS * HEAD_DIM), D_MODEL ** -0.5),
        'w_q_b': nrm(ks[13], (N_B_LAYERS, D_MODEL, B_HEADS * HEAD_DIM), D_MODEL ** -0.5),
        'w_o_b': nrm(ks[14], (N_B_LAYERS, B_SLOTS * HEAD_DIM, D_MODEL), (B_SLOTS * HEAD_DIM) ** -0.5),
        'w_gate_up': nrm(ks[15], (DEPTH, D_MODEL, 2 * D_FF), D_MODEL ** -0.5),
        'w_down': nrm(ks[16], (DEPTH, D_FF, D_MODEL), D_FF ** -0.5),
        'g_final': 1.0 + nrm(ks[17], (D_MODEL,), 0.05),
    }

def reference(x_prompt, x_sample, cache_a_k, cache_a_v, cache_b_k, cache_b_v,
              g_attn, g_ffn, w_qkv_a, sinks_a, w_o_a, g_kv, w_kv_s, w_q_b, w_o_b,
              w_gate_up, w_down, g_final):
    slopes_a = alibi_slopes(A_HEADS).reshape(A_KV_HEADS, A_GROUP)
    slopes_b = alibi_slopes(B_HEADS).reshape(B_N_GROUPS, B_SLOTS)
    wa_p = min(A_WINDOW, x_prompt.shape[1])
    wb_p = min(B_MAX_WINDOW, x_prompt.shape[1])
    wa = cache_a_k.shape[2]
    wb = cache_b_k.shape[1]
    xp, xs = x_prompt, x_sample
    bp, tp = xp.shape[:2]
    bs, ts = xs.shape[:2]
    a_k_p, a_v_p, a_k_s, a_v_s = [], [], [], []
    for l in range(DEPTH):
        if l < N_A_LAYERS:
            hp = rms_norm(xp, g_attn[l])
            hs = rms_norm(xs, g_attn[l])
            qp, kp, vp = qkv_a(hp, w_qkv_a[l])
            qs, ks_, vs_ = qkv_a(hs, w_qkv_a[l])
            sink = sinks_a[l].reshape(A_KV_HEADS, A_GROUP)
            op, _ = banded_attention(qp, kp, vp, slopes_a, 1, A_WINDOW - 1, sink)
            kcs = jnp.concatenate([cache_a_k[l], ks_], axis=1)
            vcs = jnp.concatenate([cache_a_v[l], vs_], axis=1)
            osm = window_attention_sample(qs, kcs, vcs, slopes_a, sink)
            xp = xp + op.reshape(bp, tp, A_Q_W) @ w_o_a[l]
            xs = xs + osm.reshape(bs, ts, A_Q_W) @ w_o_a[l]
            a_k_p.append(kp[:, -wa_p:])
            a_v_p.append(vp[:, -wa_p:])
            a_k_s.append(kcs[:, -wa:])
            a_v_s.append(vcs[:, -wa:])
        else:
            if l == N_A_LAYERS:
                kbp, vbp = shared_kv(xp, g_kv, w_kv_s)
                kbs, vbs = shared_kv(xs, g_kv, w_kv_s)
                kcb = jnp.concatenate([cache_b_k, kbs], axis=1)
                vcb = jnp.concatenate([cache_b_v, vbs], axis=1)
            b = l - N_A_LAYERS
            hp = rms_norm(xp, g_attn[l])
            hs = rms_norm(xs, g_attn[l])
            qp = (hp @ w_q_b[b]).reshape(bp, tp, B_N_GROUPS, B_SLOTS, HEAD_DIM)
            qs = (hs @ w_q_b[b]).reshape(bs, ts, B_N_GROUPS, B_SLOTS, HEAD_DIM)
            op = dilated_prompt(qp, kbp, vbp, slopes_b)
            osm = dilated_sample(qs, kcb, vcb, slopes_b)
            xp = xp + op.reshape(bp, tp, B_SLOTS * HEAD_DIM) @ w_o_b[b]
            xs = xs + osm.reshape(bs, ts, B_SLOTS * HEAD_DIM) @ w_o_b[b]
        xp = xp + swiglu(rms_norm(xp, g_ffn[l]), w_gate_up[l], w_down[l])
        xs = xs + swiglu(rms_norm(xs, g_ffn[l]), w_gate_up[l], w_down[l])
    y_prompt = rms_norm(xp, g_final)
    y_sample = rms_norm(xs, g_final)
    return (y_prompt, y_sample,
            jnp.stack(a_k_p, axis=0), jnp.stack(a_v_p, axis=0), kbp[:, -wb_p:], vbp[:, -wb_p:],
            jnp.stack(a_k_s, axis=0), jnp.stack(a_v_s, axis=0), kcb[:, -wb:], vcb[:, -wb:])


_drawn_inputs = setup_inputs


def setup_inputs(seed=0):
    import zlib

    import numpy as np

    out = dict(_drawn_inputs(seed))
    spreads = {}
    factors = {}
    for name, (base, spread) in spreads.items():
        noise = np.random.default_rng([zlib.crc32(name.encode()), seed]).standard_normal(out[name].shape)
        drawn = base * np.exp(spread * noise) if base else spread * noise
        out[name] = __import__('jax').numpy.asarray(drawn.astype(out[name].dtype))
    for name, factor in factors.items():
        out[name] = (out[name] * factor).astype(out[name].dtype)
    return out
```

```python
import numpy as np

import concourse.bass as bass
from concourse import mybir
from concourse.alu_op_type import AluOpType as ALU

F32 = mybir.dt.float32
F32R = mybir.dt.float32r
ACT = mybir.ActivationFunctionType

P = 128
DM = 1024
SEQ = 1024
NEWB, NEWT = 8, 8
NEW = NEWB * NEWT
TOK = SEQ + NEW
KT = DM // P
HD = 64
A_HEADS, A_KV, A_GRP = 16, 4, 4
B_SLOTS = 8
PATTERNS = ((128, 1), (512, 4), (2048, 16))
NG = len(PATTERNS)
DFF = -(-8 * DM // (3 * 256)) * 256
FT = DFF // P
PAST = 1024
EPS = 1e-6
NEG = -1e30
SCALE = HD ** -0.5
UNSCALE = 1.0 / SCALE
CH = ((0, 384), (384, 384), (768, TOK - 768))
MT = -(-TOK // P)
FCH = (6, 6, 5, 5)
UROW = B_SLOTS * HD + 2 * B_SLOTS
KEPT = 768
R16, R4, R1 = 512, 512, 128
SCOLS = R16 + R4 + R1 + NG * NEW


def phases():
    out = [("kA", 2, KT), ("vA", 2, KT), ("qA", 8, KT), ("oA", 8, KT)]
    for l in range(2):
        if l == 1:
            out += [("kB", 4, KT), ("vB", 4, KT), ("qB", 12, KT), ("oB", 8, 4)]
        for c, n in enumerate(FCH):
            out += [(f"gu{l}{c}", 2 * n, KT), (f"dn{l}{c}", 8, n)]
    return out


class Plan:

    def __init__(self):
        self.first, self.groups, self.count, self.depth, self.order = {}, {}, {}, {}, []
        s = g = 0
        for name, n, nk in phases():
            self.first[name], self.groups[name], self.count[name], self.depth[name] = s, g, n, nk
            self.order.append(name)
            s += n
            g += 0 if name[0] == "v" else n // 2

    def end(self, name):
        return self.first[name] + self.count[name]

    def next_depth(self, name):
        at = self.order.index(name) + 1
        return self.depth[self.order[at]] if at < len(self.order) else None


PLAN = Plan()


def program(nc, t):
    from contextlib import ExitStack
    ctx = ExitStack()
    with ctx:
        base = [16512]

        def at(name, shape, off, dt=F32):
            return nc.alloc_sbuf_tensor_at(name, shape, dt, offset=off)

        def take(nbytes):
            off = base[0]
            base[0] += -(-nbytes // 32) * 32
            return off

        W4 = 4 * TOK
        XT = at("XT", [P, KT * TOK], take(KT * W4))
        o_xh, o_xl = take(KT * W4 + 256), take(KT * W4 + 256)
        XH = at("XH", [P, KT * TOK + 64], o_xh, F32R)
        XL = at("XL", [P, KT * TOK + 64], o_xl, F32R)
        o_raw, o_wh, o_wl = take(8192), take(8192), take(8192)
        RAW = at("RAW", [P, 2, KT * P], o_raw)
        WH = at("WH", [P, 2, KT * P], o_wh, F32R)
        WL = at("WL", [P, 2, KT * P], o_wl, F32R)
        IDN = at("IDN", [P, P], take(512))
        ONES = at("ONES", [P, P], take(512))
        GAIN = at("GAIN", [P, 6 * KT], take(4 * 6 * KT))
        SINK = at("SINK", [P, 16], take(64))
        NSINK = at("NSINK", [P, 16], take(64))
        SINKS = at("SINKS", [P, 2], take(8))
        VAR = at("VAR", [P, MT], take(64))
        STD = at("STD", [P, MT], take(64))
        RST = at("RST", [P, MT], take(64))
        SM = at("SM", [P, 96], take(384))
        R = base[0]
        assert R + 80000 <= 229344, R
        HH = at("HH", [P, FCH[0] * TOK], R, F32R)
        HL = at("HL", [P, FCH[0] * TOK], R + FCH[0] * W4, F32R)
        GT = at("GT", [P, TOK], R + 52224)
        HT = at("HT", [P, TOK], R + 56576)
        SQ = at("SQ", [P, 2, MT * P], R + 60928)
        DIAG = at("DIAG", [P, MT, P], R + 71680)
        XNT = at("XNT", [P, 2, TOK], R + 20480)
        QA = at("QA", [P, 8 * SEQ], R)
        KA = at("KA", [P, 2 * TOK], R + 32768)
        VA = at("VA", [P, MT, 256], R + 41472)
        TABA = at("TABA", [P, 16, 256], R + 50688)
        QNA = at("QNA", [P, 8, NEW], R + 67072)
        QNS = at("QNS", [P, 2, NEWB, 32], R + 69120)
        STG = at("STG", [P, 16, P], R + 71680)
        SB = at("SB", [P, 4, 2, 256], o_wh)
        PT = at("PT", [P, 2, 512], o_wl)
        OSB = at("OSB", [P, 2, 512], o_wl + 4096)
        KCA = at("KCA", [P, NEWB, 2, P], R)
        VCA = at("VCA", [P, NEWB, 256], R + 8192)
        PSA = at("PSA", [P, NEWB, 192], R + 16384)
        PTA = at("PTA", [P, NEWB, P], R + 22528)
        PTN = at("PTN", [P, NEWB, P], R + 26624)
        TSA = at("TSA", [P, P + 120], R + 30720)
        QB = at("QB", [P, 12 * SEQ], R)
        KB = at("KB", [P, 4 * SEQ], R + 49152)
        QNB = at("QNB", [P, 12, NEW], R + 65536)
        KNB = at("KNB", [P, 4, NEW], R + 68608)
        VNB = at("VNB", [P, 512], R + 69632)
        VST = at("VST", [P, MT, 512], R)
        VG = [at("VG0", [P, 8, 512], o_xh), at("VG1", [P, 8, 512], o_xh + 16384)]
        KP = [at("KP4", [P, 4 * SEQ], o_xl), at("KP16", [P, 4 * SEQ], o_xl + 16384)]
        TAB = [at("TAB1", [P, 8, 256], o_raw), at("TAB4", [P, 8, 256], R + 49152), at("TAB16", [P, 8, P], R + 57344)]
        UST = [at("UST0", [P, UROW], o_xh + 32768), at("UST1", [P, UROW], o_xl + 32768)]
        KC = at("KC", [P, 2, 4, KEPT], R)
        VC = at("VC", [P, 2, 6, 512], R + 24576)
        SQN = at("SQN", [P, NG, 4, 32], o_xl)
        TSB = at("TSB", [P, R16 + R4 + R1], o_xl + 1536)
        TSN = at("TSN", [P, NG, NEW], o_xl + 33632)
        TSW = at("TSW", [P, NG, 120], o_xl + 6144)
        PSB = at("PSB", [P, 2, SCOLS], o_xl + 7584)
        PTS = at("PTS", [P, 7, P], o_xl + 18336)
        OM = at("OM", [P, 512], o_xl + 21920)
        PNB = at("PNB", [P, KEPT + NEW], o_xl + 23968)
        MG = [at("MG0", [P, NG, UROW], o_xl + 27296), at("MG1", [P, NG, UROW], R + 49152)]
        PS = ctx.enter_context(nc.psum_tensor("PS", [P, 8, 512], F32))

        names = """raw0 raw1 wh wl slab free0 free1 vps vev_act vev_dve const ones gain pad
            sq ssq var std rst diag rbc xnt xh xn yst0 yst1 hh hx
            stage clear score ttr exp tr pev0 pev1 pv dsink esink rl onorm0 onorm1 otr ohi olo
            tabA nsink tab1 tab4 tab16 kperm vnew vst_out vg0 vg1 ust0 ust1
            cA tsa sa_q sa_s sa_ttr sa_exp sa_es sa_p sa_tr sa_evA sa_evD sa_pv sa_out sa_outlo
            kc0 kc1 vc0 vc1 tsb sb_tab sb_stage sb_zero sb_s sb_ttr sb_exp sb_p sb_tr sb_evA sb_evD sb_pv sb_oh sb_ol
            turn mg0 mg1 m_min m_d m_w m_sum m_c m_add m_om m_tr m_hi m_lo rows_out copies""".split()
        S = {n: ctx.enter_context(nc.semaphore("s_" + n)) for n in names}
        xin = [ctx.enter_context(nc.semaphore(f"s_xin{k}")) for k in range(KT)]
        block = ctx.enter_context(nc.Block())

        ds = bass.ds

        def bank_parts(j):
            return ((PS[:, 3 * j:3 * j + 2, 0:384], 0, 768), (PS[:, 3 * j + 2:3 * j + 3, 0:CH[2][1]], 768, CH[2][1]))

        def like(ap, j_cols):
            return ap.rearrange("p (c n) -> p c n", c=2 if j_cols == 768 else 1)

        def loop(eng, lo, hi, body):
            if hi - lo == 1:
                body(lo)
            elif hi > lo:
                with eng.Fori(lo, hi, 1) as i:
                    body(i)

        def groups_done(eng, name):
            for j in range(2):
                eng.wait_ge(S[f"free{j}"], PLAN.groups[name] + PLAN.count[name] // 2)

        def keys_of(b):
            w = t["bk_in"]
            w = w[b] if isinstance(b, int) else w[ds(b, 1)].rearrange("b f k -> (b f) k")
            return w.rearrange("(c p) k -> p c k", p=P)[:, :, 0:KEPT]

        def values_of(b):
            w = t["bv_in"]
            w = w[b] if isinstance(b, int) else w[ds(b, 1)].rearrange("b k d -> (b k) d")
            return w.rearrange("(c p) d -> p c d", p=P)[:, 0:6]

        def copies(sp, c):
            sp.dma_start(t["bkS"][c], t["bk_in"][c, :, NEWT:PAST]).then_inc(S["copies"], 16)
            sp.dma_start(t["bvS"][c], t["bv_in"][c, NEWT:PAST, :]).then_inc(S["copies"], 16)
            if c == 0:
                sp.dma_start(t["akS"], t["ak_in"][:, :, NEWT:P]).then_inc(S["copies"], 16)
                sp.dma_start(t["avS"], t["av_in"][:, NEWT:P, :]).then_inc(S["copies"], 16)

        def store_u(sp, body0, dst, g):
            def body(b):
                for h in range(2):
                    sp.wait_ge(S[f"onorm{h}"], 8 + body0 + b + 1)
                    d = dst[b, h] if isinstance(b, int) else dst[ds(b, 1), h]
                    if g == 2:
                        for r in range(2):
                            dd = d[r] if isinstance(b, int) else d[:, r].rearrange("b i d -> (b i) d")
                            sp.dma_start(dd, UST[h][64 * r:64 * r + 64, :]).then_inc(S[f"ust{h}"], 16)
                    else:
                        dd = d if isinstance(b, int) else d.rearrange("b p d -> (b p) d")
                        sp.dma_start(dd, UST[h][:]).then_inc(S[f"ust{h}"], 16)
            loop(sp, 0, 4, body)

        def q_groups(eng, split, evac, plan):
            s0 = plan.first["qB"]
            for g in range(NG):
                def pair(i, last=False):
                    for j in range(2):
                        s = s0 + 4 * g + 2 * i + j
                        if not (last and g == NG - 1):
                            split(s + 2, j, KT)
                        evac(i, j, s, g)
                pair(0)
                pair(1, True)

        def store_q(copy, n, j, r, freed):
            q = QB[:, n * SEQ:(n + 1) * SEQ].rearrange("p (r i) -> p r i", r=r)
            for c, w in ((0, 384), (1, 384), (2, 256)):
                src = PS[:, 3 * j + c, 0:w].rearrange("p (i r) -> p r i", r=r)
                copy(q[:, :, 384 * c // r:(384 * c + w) // r], src)
            copy(QNB[:, n, :], PS[:, 3 * j + 2, 256:320]).then_inc(freed, 1)

        def widths_b(g):
            if g == 0:
                return lambda u, first: P if first and u < 4 else 256
            if g == 1:
                return lambda u, first: P if u < 4 else 256
            return lambda u, first: P

        def v_phase(eng, s, which, dst, is_act):
            for m in range(0 if is_act else 1, MT, 2):
                if m == MT - 1:
                    eng.wait_ge(S["slab"], s + 2)
                else:
                    eng.wait_ge(S["vps"], (MT - 1) * which + m + 1)
                copy = nc.scalar.copy if is_act else nc.vector.tensor_copy
                copy(dst(m), PS[:, m % 6, 0:256]).then_inc(S["vev_act" if is_act else "vev_dve"], 1)

        def raw_count(s, j):
            return (s - j) // 2 + 1 if isinstance(s, int) else (s - j + 2) // 2

        PLAN_H = [[1, 7, 13, 18], [23, 29, 35, 40]]

        @block.sync
        def _(sp):
            def slab(s, j, nk, src):
                if not (isinstance(s, int) and s < 2):
                    sp.wait_ge(S["wh"], s - 1)
                    sp.wait_ge(S["wl"], s - 1)
                sp.dma_start(RAW[:, j, 0:nk * P], src).then_inc(S[f"raw{j}"], 16)

            def slabs(name, w, skip=0):
                s0, n, nk = PLAN.first[name], PLAN.count[name], PLAN.depth[name]

                def pair(i):
                    for j in range(2):
                        src = w[2 * i + j] if isinstance(i, int) else w[ds(2 * i + j, 1)].rearrange("a p n -> (a p) n")
                        slab(s0 + 2 * i + j, j, nk, src)
                loop(sp, skip, n // 2, pair)

            for k in range(KT):
                sp.dma_start(XT[:, k * TOK:(k + 1) * TOK], t["xT"][k]).then_inc(xin[k], 16)
            sp.dma_start(IDN[:], t["ident"]).then_inc(S["const"], 16)
            sp.dma_start(GAIN[:], t["gains"]).then_inc(S["gain"], 16)
            slabs("kA", t["w_kA"])
            slabs("vA", t["w_vA"])
            sp.wait_ge(S["ssq"], KT)
            sp.dma_start(TABA[:], t["tabA"]).then_inc(S["tabA"], 16)
            sp.dma_start(SINK[:], t["sinks"]).then_inc(S["tabA"], 16)
            slabs("qA", t["w_qA"])
            sp.wait_ge(S["stage"], 64)
            for a in range(2):
                sp.dma_start(KCA[:, :, a, :], t["ak_in"].rearrange("b (a p) k -> a p b k", a=2)[a]).then_inc(S["cA"], 16)
            sp.dma_start(VCA[:], t["av_in"].rearrange("b k d -> k b d")).then_inc(S["cA"], 16)
            sp.dma_start(TSA[:], t["tabSA"]).then_inc(S["tsa"], 16)
            sp.dma_start(SINKS[:, 0:1], t["sinkS"]).then_inc(S["tsa"], 16)
            slabs("oA", t["w_oA"])
            for c in range(len(FCH)):
                copies(sp, c)
                slabs(f"gu0{c}", t[f"w_gu0{c}"])
                slabs(f"dn0{c}", t[f"w_dn0{c}"])
            slabs("kB", t["w_kB"])
            slabs("vB", t["w_vB"])
            slabs("qB", t["w_qB"])
            sp.wait_ge(S["wl"], PLAN.end("qB"))
            sp.dma_start(TAB[0][:], t["tabB1"]).then_inc(S["tab1"], 16)
            sp.wait_ge(S["slab"], PLAN.end("qB"))
            sp.wait_ge(S["vst_out"], 32)
            vrow = t["bv"]
            sp.dma_start(VG[0][:], vrow[0:SEQ].rearrange("(n p) d -> p n d", p=P)).then_inc(S["vg0"], 16)
            v4 = vrow[0:SEQ].rearrange("(c p r) d -> r p c d", r=4, p=P)
            for r in range(4):
                sp.dma_start(VG[1][:, 2 * r:2 * r + 2, :], v4[r]).then_inc(S["vg1"], 16)
            store_u(sp, 0, t["u"][0].rearrange("(b h p) d -> b h p d", h=2, p=P), 0)
            sp.wait_ge(S["score"], 64 + 32)
            sp.wait_ge(S["kperm"], 8)
            sp.wait_ge(S["rows_out"], 80)
            sp.dma_start(TAB[1][:], t["tabB4"]).then_inc(S["tab4"], 16)
            sp.dma_start(TAB[2][:], t["tabB16"]).then_inc(S["tab16"], 16)
            sp.wait_ge(S["pv"], 64 + 32)
            v16 = vrow[0:SEQ].rearrange("(i n r) d -> r i n d", r=2, n=8)
            for r in range(2):
                sp.dma_start(VG[0][64 * r:64 * r + 64, :, :], v16[r]).then_inc(S["vg0"], 16)
            store_u(sp, 4, t["u"][1].rearrange("(h p b) d -> b h p d", h=2, b=4), 1)
            store_u(sp, 8, t["u"][2].rearrange("(i b h r) d -> b h r i d", r=2, h=2, b=4), 2)
            sp.wait_ge(S["stage"], 64 + 96)
            sp.wait_ge(S["score"], 64 + 96)
            sp.dma_start(TSB[:], t["tabSB"]).then_inc(S["tsb"], 16)
            sp.dma_start(TSW[:], t["tabSW"]).then_inc(S["tsb"], 16)
            sp.wait_ge(S["ust0"], 16 * 16)
            sp.wait_ge(S["ust1"], 16 * 16)

            def sample_loads(i):
                for j in range(2):
                    b = 2 * i + j
                    if not (isinstance(i, int) and i == 0):
                        sp.wait_ge(S["sb_s"], 2 * i + j - 1)
                    sp.dma_start(KC[:, j], keys_of(b)).then_inc(S[f"kc{j}"], 16)
                    if not (isinstance(i, int) and i == 0):
                        sp.wait_ge(S["sb_pv"], 2 * i + j - 1)
                    sp.dma_start(VC[:, j], values_of(b)).then_inc(S[f"vc{j}"], 16)
                    if not (isinstance(i, int) and i == 0):
                        sp.wait_ge(S["m_om"], 2 * i + j - 1)
                    src = t["u"][:, ds(b * P, P), :].rearrange("g p d -> p g d")
                    sp.dma_start(MG[j][:], src).then_inc(S[f"mg{j}"], 16)
            sample_loads(0)
            loop(sp, 1, 4, sample_loads)
            slabs("oB", t["w_oB"])
            for c in range(len(FCH)):
                copies(sp, 4 + c)
                slabs(f"gu1{c}", t[f"w_gu1{c}"])
                slabs(f"dn1{c}", t[f"w_dn1{c}"])
            for k in range(KT):
                sp.wait_ge(S["xnt"], 5 * KT + k + 1)
                sp.dma_start(t["yT"][k], XNT[:, k % 2, :]).then_inc(S[f"yst{k % 2}"], 16)
            sp.wait_ge(S["yst0"], 64)
            sp.wait_ge(S["yst1"], 64)
            sp.wait_ge(S["copies"], 16 * 18)
            sp.wait_ge(S["rows_out"], 16 * 5)

        @block.gpsimd
        def _(pool):
            nc.gpsimd.memset(ONES[:], 1.0).then_inc(S["ones"], 1)

            def stage(src, u):
                for kk in range(2):
                    r = slice(64 * kk, 64 * kk + 64)
                    ins = nc.gpsimd.tensor_copy(STG[r, 2 * u + kk, :], src[r])
                ins.then_inc(S["stage"], 1)

            def clear_stage(n):
                nc.gpsimd.memset(STG[:], 0.0).then_inc(S["clear"], 1)
                pool.wait_ge(S["clear"], n)

            def stage_a(i, first=False):
                for u in range(8):
                    if not first:
                        pool.wait_ge(S["score"], 8 * i + u - 7)
                    stage(QA[:, ds(u * SEQ + i * P, P)], u)

            groups_done(pool, "kA")
            ka = KA[:].rearrange("p (a n) -> p a n", a=2)
            pool.dma_start(t["akT"], ka[:, :, SEQ - P:TOK]).then_inc(S["rows_out"], 16)
            pool.wait_ge(S["vev_act"], 5)
            pool.wait_ge(S["vev_dve"], 4)
            pool.dma_start(t["avN"][0:P], VA[:, 7, :]).then_inc(S["rows_out"], 16)
            pool.dma_start(t["avN"][P:P + NEW], VA[0:NEW, 8, :]).then_inc(S["rows_out"], 16)
            groups_done(pool, "qA")
            clear_stage(1)
            stage_a(0, True)
            loop(pool, 1, 8, stage_a)
            groups_done(pool, "kB")
            pool.dma_start(t["bkT"], KB[:]).then_inc(S["rows_out"], 16)
            pool.dma_start(t["bkN"], KNB[:]).then_inc(S["rows_out"], 16)
            pool.wait_ge(S["vev_act"], 15)
            pool.wait_ge(S["vev_dve"], 12)
            pool.dma_start(t["bv"][0:SEQ].rearrange("(n p) d -> p n d", p=P), VST[:, 0:8, :]).then_inc(S["vst_out"], 16)
            pool.dma_start(t["bv"][SEQ:TOK], VST[0:NEW, 8, :]).then_inc(S["vst_out"], 16)
            groups_done(pool, "qB")
            clear_stage(2)

            def stage_b(g, i, first=False):
                for u in range(8):
                    if not first:
                        pool.wait_ge(S["score"], 64 + 32 * g + 8 * i + u - 7)
                    stage(QB[:, ds((4 * g + u % 4) * SEQ + (2 * i + u // 4) * P, P)], u)
            stage_b(0, 0, True)
            pool.wait_ge(S["slab"], PLAN.end("qB"))
            pool.wait_ge(S["stage"], 64 + 8)
            for x, r in enumerate((4, 16)):
                for p in range(4):
                    nc.gpsimd.tensor_copy(KP[x][:, p * SEQ:(p + 1) * SEQ].rearrange("p (r i) -> p r i", r=r),
                                          KB[:, p * SEQ:(p + 1) * SEQ].rearrange("p (i r) -> p r i", r=r)).then_inc(S["kperm"], 1)

            pool.wait_ge(S["kperm"], 8)
            for g in range(NG):
                loop(pool, 0 if g else 1, 4, lambda i: stage_b(g, i))
            pool.wait_ge(S["score"], 64 + 96)
            pool.wait_ge(S["stage"], 64 + 96)
            nc.gpsimd.memset(SQN[:], 0.0).then_inc(S["sb_zero"], 1)
            pool.wait_ge(S["sb_zero"], 1)

            def sample(b, first, merged=None):
                if not first:
                    pool.wait_ge(S["sb_s"], b)
                if merged is not None:
                    pool.wait_ge(S["m_om"], merged)
                for kk in range(2):
                    src = QNB[64 * kk:64 * kk + 64, :, ds(b * NEWT, NEWT)]
                    dst = SQN[64 * kk:64 * kk + 64, :, :, 8 * kk:8 * kk + 8].rearrange("p g a n -> p (g a) n")
                    nc.gpsimd.tensor_copy(dst, src).then_inc(S["sb_stage"], 1)

            def merge(b, j, staged):
                pool.wait_ge(S["sb_stage"], 2 * staged)
                pool.wait_ge(S["m_c"], b + 1)
                c = SM[:, 64:88].unsqueeze(2).to_broadcast([P, 24, HD])
                for g in range(NG):
                    u = MG[j][:, g, 0:512].rearrange("p (h d) -> p h d", h=8)
                    nc.gpsimd.tensor_tensor(u, u, c[:, 8 * g:8 * g + 8, :], ALU.mult).then_inc(S["m_add"], 1)
                pool.wait_ge(S["m_add"], 4 * b + 3)
                nc.gpsimd.tensor_tensor(MG[j][:, 0, 0:512], MG[j][:, 0, 0:512], MG[j][:, 1, 0:512], ALU.add).then_inc(S["m_add"], 1)
                pool.wait_ge(S["m_add"], 4 * b + 4)
                if not (isinstance(b, int) and b == 0):
                    pool.wait_ge(S["m_tr"], b)
                nc.gpsimd.tensor_tensor(OM[:], MG[j][:, 0, 0:512], MG[j][:, 2, 0:512], ALU.add).then_inc(S["m_om"], 1)

            sample(0, True)
            sample(1, False)
            merge(0, 0, 2)
            sample(2, False, 1)
            merge(1, 1, 3)

            def pair(i):
                sample(2 * i + 1, False, 2 * i)
                merge(2 * i, 0, 2 * i + 2)
                sample(2 * i + 2, False, 2 * i + 1)
                merge(2 * i + 1, 1, 2 * i + 3)
            loop(pool, 1, 3, pair)
            sample(7, False, 6)
            merge(6, 0, 8)
            merge(7, 1, 8)

        @block.scalar
        def _(act):
            def split_hi(s, j, nk):
                if not (isinstance(s, int) and s < 2):
                    act.wait_ge(S["slab"], s - 1)
                act.wait_ge(S[f"raw{j}"], 16 * raw_count(s, j))
                nc.scalar.copy(WH[:, j, 0:nk * P], RAW[:, j, 0:nk * P]).then_inc(S["wh"], 1)

            def t_phase(name, evac, prefetch=True, square=None):
                s0, n, nk = PLAN.first[name], PLAN.count[name], PLAN.depth[name]

                def pair(i, last=False):
                    for j in range(2):
                        s = s0 + 2 * i + j
                        if not last:
                            split_hi(s + 2, j, nk)
                        elif prefetch and PLAN.next_depth(name):
                            split_hi(s + 2, j, PLAN.next_depth(name))
                        if evac:
                            evac(i, j, s)
                loop(act, 0, n // 2 - 1, pair)
                pair(n // 2 - 1, True)

            def start(name):
                nk = PLAN.depth[name]
                for j in range(2):
                    split_hi(PLAN.first[name] + j, j, nk)

            def squares(norm, k, j, source, count):
                act.wait_ge(source, count)
                q = KT * norm + k
                if not (isinstance(k, int) and q < 2):
                    act.wait_ge(S["ssq"], q - 1)
                nc.scalar.activation(SQ[:, j, 0:TOK], XT[:, ds(k * TOK, TOK)], ACT.Square).then_inc(S["sq"], 1)

            def sqrt_var(norm):
                act.wait_ge(S["var"], norm + 1)
                nc.scalar.activation(STD[:], VAR[:], ACT.Sqrt).then_inc(S["std"], 1)

            def norm_hi(x, before):
                if before:
                    act.wait_ge(S["slab"], before)
                for k in range(KT):
                    act.wait_ge(S["xnt"], KT * x + k + 1)
                    nc.scalar.copy(XH[:, k * TOK:(k + 1) * TOK], XNT[:, k % 2, :]).then_inc(S["xh"], 1)

            start("kA")
            for k in range(KT):
                squares(0, k, k % 2, xin[k], 16)
            sqrt_var(0)
            norm_hi(0, 0)

            def evac_kA(i, j, s):
                if j == 0:
                    act.wait_ge(S["slab"], s + 1)
                    for ps, off, w in bank_parts(0):
                        ins = nc.scalar.copy(like(KA[:, off:off + w], w), ps)
                    ins.then_inc(S["free0"], 1)
            t_phase("kA", evac_kA)
            v_phase(act, PLAN.first["vA"], 0, lambda m: VA[:, m, :], True)
            for j in range(2):
                split_hi(PLAN.first["qA"] + j, j, KT)

            def evac_rows(dst, new):
                def evac(i, j, s):
                    if j == 0:
                        act.wait_ge(S["slab"], s + 1)
                        n = 2 * i
                        nc.scalar.copy(like(dst[:, ds(n * SEQ, 768)], 768), PS[:, 0:2, 0:384])
                        nc.scalar.copy(dst[:, ds(n * SEQ + 768, 256)], PS[:, 2, 0:256])
                        nc.scalar.copy(new[:, ds(n, 1), :], PS[:, 2:3, 256:320]).then_inc(S["free0"], 1)
                return evac
            t_phase("qA", evac_rows(QA, QNA), prefetch=False)

            def attention(units0, n_bodies, peel, widths, finish):
                def exp_unit(i, u, w):
                    U = units0 + 8 * i + u
                    act.wait_ge(S["ttr"], U + 1)
                    for kk in range(2):
                        h = 2 * u + kk
                        ins = nc.scalar.activation(SB[:, u % 4, kk, 0:w], SB[:, u % 4, kk, 0:w], ACT.Exp,
                                                   bias=SM[:, h:h + 1], scale=-1.0, accum_out=SM[:, 16 + h:17 + h])
                    ins.then_inc(S["exp"], 1)

                def evac(i, u, w):
                    U = units0 + 8 * i + u
                    act.wait_ge(S["tr"], U + 1)
                    if not (isinstance(U, int) and U < 2):
                        act.wait_ge(S["pv"], U - 1)
                    nc.scalar.copy(PT[:, 1, 0:2 * w], PS[:, 3, 0:2 * w]).then_inc(S["pev1"], 1)

                def body(i, prev, cur=True, first=False, prev_first=False):
                    for st in range(8):
                        if cur:
                            exp_unit(i, st, widths(st, first))
                        v = (st - 2) % 8
                        if v % 2 == 1 and (st >= 2 and cur):
                            evac(i, v, widths(v, first))
                        if v % 2 == 1 and st < 2 and prev is not None:
                            evac(prev, v, widths(v, prev_first))
                        if finish:
                            finish(i, prev, st, cur)
                body(0, None, first=True)
                if peel:
                    body(1, 0, prev_first=True)
                loop(act, 1 + peel, n_bodies, lambda i: body(i, i - 1))
                body(n_bodies, n_bodies - 1, cur=False)

            def finish_a(i, prev, st, cur):
                def es(b, h):
                    act.wait_ge(S["dsink"], 2 * b + h + 1)
                    nc.scalar.activation(SM[:, 48 + 8 * h:56 + 8 * h], SM[:, 32 + 8 * h:40 + 8 * h], ACT.Exp).then_inc(S["esink"], 1)

                def hi(b, h):
                    act.wait_ge(S["otr"], 2 * b + h + 1)
                    dst = XH[:, 0:KT * TOK].rearrange("p (k n) -> p k n", k=KT)[:, 4 * h:4 * h + 4, ds(b * P, P)]
                    nc.scalar.copy(dst, PS[:, 6 + h, :].rearrange("p (k n) -> p k n", k=4)).then_inc(S["ohi"], 1)
                if st == 4 and cur:
                    es(i, 0)
                if st == 0 and prev is not None:
                    es(prev, 1)
                    hi(prev, 0)
                if st == 4 and prev is not None:
                    hi(prev, 1)

            act.wait_ge(S["slab"], PLAN.end("qA"))
            attention(0, 8, 1, lambda u, first: P if first else 256, finish_a)

            act.wait_ge(S["tsa"], 32)
            for b in range(NEWB):
                act.wait_ge(S["sa_ttr"], 2 * b + 2)
                nc.scalar.activation(PSA[:, b, :], PSA[:, b, :], ACT.Exp, bias=SM[:, b:b + 1], scale=-1.0,
                                     accum_out=SM[:, 16 + b:17 + b]).then_inc(S["sa_exp"], 1)
            nc.scalar.activation(SM[:, 32:40], SM[:, 0:8], ACT.Exp, bias=SINKS[:, 0:1]).then_inc(S["sa_es"], 1)
            for q in range(2):
                act.wait_ge(S["sa_tr"], q + 1)
                nc.scalar.copy(PTA[:, 4 * q:4 * q + 4, :], PS[:, 2 + q, :].rearrange("p (b n) -> p b n", b=4)).then_inc(S["sa_evA"], 1)
            for a in range(2):
                act.wait_ge(S["sa_pv"], a + 1)
                for kk in range(2):
                    src = PS[64 * kk:64 * kk + 64, 6 + a, :].rearrange("p (b k g i) -> p k g b i", b=8, k=2, g=4)[:, kk]
                    dst = XH[64 * kk:64 * kk + 64, 0:KT * TOK].rearrange("p (k n) -> p k n", k=KT)[:, 4 * a:4 * a + 4, SEQ:TOK]
                    nc.scalar.copy(dst.rearrange("p g (b i) -> p g b i", b=8), src).then_inc(S["sa_out"], 1)

            def evac_sq(norm, name):
                def evac(i, j, s):
                    squares(norm, 2 * i + j, j, S[f"free{j}"], PLAN.groups[name] + i + 1)
                return evac
            act.wait_ge(S["pv"], 64)
            start("oA")
            t_phase("oA", evac_sq(1, "oA"))
            sqrt_var(1)
            norm_hi(1, PLAN.end("oA"))
            act.wait_ge(S["rows_out"], 48)

            def ffn(l):
                for c, nf in enumerate(FCH):
                    fill0 = PLAN.groups[f"gu{l}{c}"]

                    def evac_gu(i, j, s, fill0=fill0):
                        if j == 0:
                            act.wait_ge(S["slab"], s + 1)
                            act.wait_ge(S["free1"], fill0 + i)
                            for ps, off, w in bank_parts(0):
                                ins = nc.scalar.activation(like(GT[:, off:off + w], w), ps, ACT.Silu)
                            ins.then_inc(S["free0"], 1)
                        else:
                            act.wait_ge(S["free1"], fill0 + i + 1)
                            nc.scalar.copy(HH[:, ds(i * TOK, TOK)], HT[:]).then_inc(S["hh"], 1)
                    t_phase(f"gu{l}{c}", evac_gu)
                    if c == len(FCH) - 1:
                        t_phase(f"dn{l}{c}", evac_sq(2 + 2 * l, f"dn{l}{c}"))
                    else:
                        t_phase(f"dn{l}{c}", None)
            ffn(0)
            sqrt_var(2)
            norm_hi(2, PLAN.end("dn03"))

            t_phase("kB", evac_rows(KB, KNB))
            for q in range(2):
                v_phase(act, PLAN.first["vB"] + 2 * q, 1 + q, lambda m: VST[:, m, 256 * q:256 * q + 256], True)
                for j in range(2):
                    split_hi(PLAN.first["vB"] + 2 * q + 2 + j, j, KT)
            norm_hi(3, PLAN.end("vB"))

            def evac_qB(i, j, s, g):
                if j == 0:
                    act.wait_ge(S["slab"], s + 1)
                    n = 4 * g + 2 * i
                    store_q(nc.scalar.copy, n, 0, PATTERNS[g][1], S["free0"])
            act.wait_ge(S["vst_out"], 32)
            act.wait_ge(S["vnew"], 1)
            q_groups(act, split_hi, evac_qB, PLAN)

            act.wait_ge(S["slab"], PLAN.end("qB"))
            for g in range(NG):
                attention(64 + 32 * g, 4, 0, widths_b(g), None)

            def sample(b, j):
                act.wait_ge(S["sb_ttr"], 4 * b + 4)
                nc.scalar.activation(PSB[:, j, :], PSB[:, j, :], ACT.Exp, bias=SM[:, 3:4], scale=-1.0,
                                     accum_out=SM[:, 8:9]).then_inc(S["sb_exp"], 1)

            def merge_w(b, j):
                act.wait_ge(S["m_d"], b + 1)
                nc.scalar.activation(SM[:, 40:64], SM[:, 40:64], ACT.Exp).then_inc(S["m_w"], 1)

            def sample_out(b):
                act.wait_ge(S["sb_tr"], 2 * b + 1)
                if not (isinstance(b, int) and b == 0):
                    act.wait_ge(S["sb_pv"], b)
                nc.scalar.copy(PTS[:, 0:4, :], PS[:, 5, :].rearrange("p (c n) -> p c n", c=4)).then_inc(S["sb_evA"], 1)
                act.wait_ge(S["sb_pv"], b + 1)
                for kk in range(2):
                    src = PS[64 * kk:64 * kk + 64, 7, 0:128].rearrange("p (a n) -> p a n", a=4)[:, :, 8 * kk:8 * kk + 8]
                    dst = XH[64 * kk:64 * kk + 64, 0:4 * TOK].rearrange("p (k n) -> p k n", k=4)[:, :, ds(SEQ + b * NEWT, NEWT)]
                    nc.scalar.copy(dst, src).then_inc(S["sb_oh"], 1)

            def merge_out(b):
                act.wait_ge(S["m_tr"], b + 1)
                dst = XH[:, 0:4 * TOK].rearrange("p (k n) -> p k n", k=4)[:, :, ds(b * P, P)]
                nc.scalar.copy(dst, PS[:, 0, :].rearrange("p (k n) -> p k n", k=4)).then_inc(S["m_hi"], 1)

            def batch(b, j, first=False, last=False):
                if not last:
                    merge_w(b, j)
                    sample(b, j)
                if not first:
                    sample_out(b - 1)
                    merge_out(b - 1)
            batch(0, 0, first=True)
            batch(1, 1)

            def pair(i):
                batch(2 * i, 0)
                batch(2 * i + 1, 1)
            loop(act, 1, 4, pair)
            batch(8, 0, last=True)

            act.wait_ge(S["rows_out"], 80)
            start("oB")
            t_phase("oB", evac_sq(3, "oB"))
            sqrt_var(3)
            norm_hi(4, PLAN.end("oB"))
            ffn(1)
            sqrt_var(4)

        @block.vector
        def _(dve):
            def split_lo(s, j, nk):
                dve.wait_ge(S["wh"], s + 1)
                nc.vector.tensor_tensor(WL[:, j, 0:nk * P], RAW[:, j, 0:nk * P], WH[:, j, 0:nk * P].bitcast(F32),
                                        ALU.subtract).then_inc(S["wl"], 1)

            def t_phase(name, evac, prefetch=True):
                s0, n, nk = PLAN.first[name], PLAN.count[name], PLAN.depth[name]

                def pair(i, last=False):
                    for j in range(2):
                        s = s0 + 2 * i + j
                        if not last:
                            split_lo(s + 2, j, nk)
                        elif prefetch and PLAN.next_depth(name):
                            split_lo(s + 2, j, PLAN.next_depth(name))
                        if evac:
                            evac(i, j, s)
                loop(dve, 0, n // 2 - 1, pair)
                pair(n // 2 - 1, True)

            def start(name):
                for j in range(2):
                    split_lo(PLAN.first[name] + j, j, PLAN.depth[name])

            def pad():
                nc.vector.memset(SQ[:, :, TOK:], 0.0).then_inc(S["pad"], 1)

            def rstd(norm):
                dve.wait_ge(S["ssq"], KT * (norm + 1))
                nc.vector.tensor_scalar(VAR[:], PS[:, 6, 0:MT], 1.0 / DM, EPS, ALU.mult, ALU.add).then_inc(S["var"], 1)
                dve.wait_ge(S["std"], norm + 1)
                nc.vector.reciprocal(RST[:], STD[:]).then_inc(S["rst"], 1)
                dve.wait_ge(S["rst"], norm + 1)
                if norm == 0:
                    dve.wait_ge(S["const"], 16)
                nc.vector.tensor_tensor(DIAG[:], IDN[:].unsqueeze(1).to_broadcast([P, MT, P]),
                                        RST[:].unsqueeze(2).to_broadcast([P, MT, P]), ALU.mult).then_inc(S["diag"], 1)

            def norm_tiles(x, gain, final=False):
                if x == 0:
                    dve.wait_ge(S["gain"], 16)
                dve.wait_ge(S["rbc"], x + 1)
                for k in range(KT + 1):
                    if k < KT:
                        if final and k >= 2:
                            dve.wait_ge(S[f"yst{k % 2}"], 16 * (k // 2))
                        elif k >= 2:
                            dve.wait_ge(S["xn"], KT * x + k - 1)
                        g = GAIN[:, gain * KT + k:gain * KT + k + 1]
                        for n, (ps, off, w) in enumerate(bank_parts(1)):
                            ins = nc.vector.scalar_tensor_tensor(
                                like(XNT[:, k % 2, off:off + w], w), like(XT[:, k * TOK + off:k * TOK + off + w], w),
                                g, ps, ALU.mult, ALU.mult)
                        ins.then_inc(S["xnt"], 1)
                    if k >= 1 and not final:
                        q = k - 1
                        dve.wait_ge(S["xh"], KT * x + k)
                        nc.vector.tensor_tensor(XL[:, q * TOK:(q + 1) * TOK], XNT[:, q % 2, :],
                                                XH[:, q * TOK:(q + 1) * TOK].bitcast(F32), ALU.subtract).then_inc(S["xn"], 1)

            nc.vector.memset(XH[:, KT * TOK:].bitcast(F32), 0.0)
            nc.vector.memset(XL[:, KT * TOK:].bitcast(F32), 0.0)
            pad()
            start("kA")
            rstd(0)
            norm_tiles(0, 0)

            def evac_kA(i, j, s):
                if j == 1:
                    dve.wait_ge(S["slab"], s + 1)
                    for ps, off, w in bank_parts(1):
                        ins = nc.vector.tensor_copy(like(KA[:, TOK + off:TOK + off + w], w), ps)
                    ins.then_inc(S["free1"], 1)
            t_phase("kA", evac_kA)
            v_phase(dve, PLAN.first["vA"], 0, lambda m: VA[:, m, :], False)
            for j in range(2):
                split_lo(PLAN.first["qA"] + j, j, KT)

            def evac_rows(dst, new):
                def evac(i, j, s):
                    if j == 1:
                        dve.wait_ge(S["slab"], s + 1)
                        n = 2 * i + 1
                        nc.vector.tensor_copy(like(dst[:, ds(n * SEQ, 768)], 768), PS[:, 3:5, 0:384])
                        nc.vector.tensor_copy(dst[:, ds(n * SEQ + 768, 256)], PS[:, 5, 0:256])
                        nc.vector.tensor_copy(new[:, ds(n, 1), :], PS[:, 5:6, 256:320]).then_inc(S["free1"], 1)
                return evac
            t_phase("qA", evac_rows(QA, QNA), prefetch=False)

            def attention(units0, n_bodies, peel, widths, table, loaded, init, norm, extra):
                def scores(i, u, w):
                    U = units0 + 8 * i + u
                    dve.wait_ge(S["score"], U + 1)
                    if not (isinstance(U, int) and U < 4):
                        dve.wait_ge(S["tr"], U - 3)
                    if u % 4 == 0 and not (isinstance(i, int) and units0 + i == 0):
                        dve.wait_ge(S[f"onorm{u // 4}"], units0 // 8 + i)
                    dve.wait_ge(S[loaded], 16)
                    dve.sem_inc(S["turn"], 1)
                    for kk in range(2):
                        h = 2 * u + kk
                        ins = nc.vector.tensor_tensor_reduce(
                            out=SB[:, u % 4, kk, 0:w], in0=PS[:, u % 2, kk * w:(kk + 1) * w], in1=table(u, kk, w),
                            scale=-SCALE, scalar=init(h), op0=ALU.add, op1=ALU.min, accum_out=SM[:, h:h + 1])
                    ins.then_inc(S["ttr"], 1)

                def evac(i, u, w):
                    U = units0 + 8 * i + u
                    dve.wait_ge(S["tr"], U + 1)
                    if not (isinstance(U, int) and U < 2):
                        dve.wait_ge(S["pv"], U - 1)
                    nc.vector.tensor_copy(PT[:, 0, 0:2 * w], PS[:, 2, 0:2 * w]).then_inc(S["pev0"], 1)

                def body(i, prev, cur=True, first=False, prev_first=False):
                    for st in range(8):
                        if cur:
                            scores(i, st, widths(st, first))
                        v = (st - 2) % 8
                        if v % 2 == 0 and st >= 2 and cur:
                            evac(i, v, widths(v, first))
                        if v % 2 == 0 and st < 2 and prev is not None:
                            evac(prev, v, widths(v, prev_first))
                        if st == 6 and cur:
                            norm(i, 0)
                        if st == 2 and prev is not None:
                            norm(prev, 1)
                        if extra:
                            extra(i, prev, st, cur)
                body(0, None, first=True)
                if peel:
                    body(1, 0, prev_first=True)
                loop(dve, 1 + peel, n_bodies, lambda i: body(i, i - 1))
                body(n_bodies, n_bodies - 1, cur=False)

            def norm_a(b, h):
                dve.wait_ge(S["esink"], 2 * b + h + 1)
                lo = 8 * h
                nc.vector.tensor_tensor(SM[:, 64 + lo:72 + lo], SM[:, 16 + lo:24 + lo], SM[:, 48 + lo:56 + lo], ALU.add).then_inc(S["rl"], 1)
                dve.wait_ge(S["rl"], 4 * b + 2 * h + 1)
                nc.vector.reciprocal(SM[:, 80 + lo:88 + lo], SM[:, 64 + lo:72 + lo]).then_inc(S["rl"], 1)
                dve.wait_ge(S["rl"], 4 * b + 2 * h + 2)
                dve.wait_ge(S["pv"], 8 * b + 4 * h + 4)
                if not (isinstance(b, int) and b == 0):
                    dve.wait_ge(S["otr"], 2 * b + h - 1)
                nc.vector.tensor_tensor(OSB[:, h, :].rearrange("p (a d) -> p a d", a=8),
                                        PS[:, 4 + h, :].rearrange("p (a d) -> p a d", a=8),
                                        SM[:, 80 + lo:88 + lo].unsqueeze(2).to_broadcast([P, 8, HD]),
                                        ALU.mult).then_inc(S[f"onorm{h}"], 1)

            def extra_a(i, prev, st, cur):
                def dsink(b, h):
                    lo = 8 * h
                    dve.wait_ge(S["ttr"], 8 * b + 4 * h + 4)
                    nc.vector.tensor_tensor(SM[:, 32 + lo:40 + lo], SM[:, lo:lo + 8], NSINK[:, lo:lo + 8],
                                            ALU.subtract).then_inc(S["dsink"], 1)

                def lo_part(b, h):
                    dve.wait_ge(S["ohi"], 2 * b + h + 1)
                    xl = XL[:, 0:KT * TOK].rearrange("p (k n) -> p k n", k=KT)[:, 4 * h:4 * h + 4, ds(b * P, P)]
                    xh = XH[:, 0:KT * TOK].rearrange("p (k n) -> p k n", k=KT)[:, 4 * h:4 * h + 4, ds(b * P, P)]
                    nc.vector.tensor_tensor(xl, PS[:, 6 + h, :].rearrange("p (k n) -> p k n", k=4),
                                            xh.bitcast(F32), ALU.subtract).then_inc(S["olo"], 1)
                if st == 3 and cur:
                    dsink(i, 0)
                if st == 7 and cur:
                    dsink(i, 1)
                if st == 1 and prev is not None:
                    lo_part(prev, 0)
                if st == 5 and prev is not None:
                    lo_part(prev, 1)

            dve.wait_ge(S["tabA"], 32)
            nc.vector.tensor_scalar(NSINK[:], SINK[:], -1.0, None, ALU.mult).then_inc(S["nsink"], 1)
            dve.wait_ge(S["nsink"], 1)
            dve.wait_ge(S["slab"], PLAN.end("qA"))
            attention(0, 8, 1, lambda u, first: P if first else 256,
                      lambda u, kk, w: TABA[:, 2 * u + kk, 256 - w:256], "tabA", lambda h: NSINK[:, h:h + 1], norm_a, extra_a)

            dve.wait_ge(S["tsa"], 32)
            nc.vector.tensor_scalar(SINKS[:, 1:2], SINKS[:, 0:1], -1.0, None, ALU.mult).then_inc(S["nsink"], 1)
            dve.wait_ge(S["nsink"], 2)
            dve.wait_ge(S["stage"], 64)
            for a in range(2):
                nc.vector.tensor_copy(QNS[:, a].rearrange("p b (g i) -> p b g i", g=4),
                                      QNA[:, 4 * a:4 * a + 4, :].rearrange("p g (b i) -> p b g i", b=NEWB)).then_inc(S["sa_q"], 1)
            for b in range(NEWB):
                dve.wait_ge(S["sa_s"], b + 1)
                nc.vector.tensor_tensor_reduce(out=PSA[:, b, 0:P], in0=PS[:, b % 2, 0:P], in1=TSA[:, 0:P], scale=-SCALE,
                                               scalar=SINKS[:, 1:2], op0=ALU.add, op1=ALU.min,
                                               accum_out=SM[:, 8 + b:9 + b]).then_inc(S["sa_ttr"], 1)
                dve.wait_ge(S["sa_ttr"], 2 * b + 1)
                w0 = P + 56 - 8 * b
                nc.vector.tensor_tensor_reduce(out=PSA[:, b, P:192], in0=PS[:, b % 2, P:192], in1=TSA[:, w0:w0 + 64],
                                               scale=-SCALE, scalar=SM[:, 8 + b:9 + b], op0=ALU.add, op1=ALU.min,
                                               accum_out=SM[:, b:b + 1]).then_inc(S["sa_ttr"], 1)
            dve.wait_ge(S["sa_es"], 1)
            nc.vector.tensor_tensor(SM[:, 40:48], SM[:, 16:24], SM[:, 32:40], ALU.add).then_inc(S["sa_p"], 1)
            dve.wait_ge(S["sa_p"], 1)
            nc.vector.reciprocal(SM[:, 48:56], SM[:, 40:48]).then_inc(S["sa_p"], 1)
            dve.wait_ge(S["sa_p"], 2)
            nc.vector.tensor_tensor(PSA[:], PSA[:], SM[:, 48:56].unsqueeze(2).to_broadcast([P, NEWB, 192]),
                                    ALU.mult).then_inc(S["sa_p"], 1)
            for q in range(2):
                dve.wait_ge(S["sa_tr"], 3 + q)
                nc.vector.tensor_copy(PTN[0:64, 4 * q:4 * q + 4, :], PS[0:64, 4 + q, :].rearrange("p (b n) -> p b n", b=4)).then_inc(S["sa_evD"], 1)
            for a in range(2):
                for kk in range(2):
                    dve.wait_ge(S["sa_out"], 2 * a + kk + 1)
                    src = PS[64 * kk:64 * kk + 64, 6 + a, :].rearrange("p (b k g i) -> p k g b i", b=8, k=2, g=4)[:, kk]
                    xh, xl = (X[64 * kk:64 * kk + 64, 0:KT * TOK].rearrange("p (k n) -> p k n", k=KT)[:, 4 * a:4 * a + 4, SEQ:TOK]
                              .rearrange("p g (b i) -> p g b i", b=8) for X in (XH, XL))
                    nc.vector.tensor_tensor(xl, src, xh.bitcast(F32), ALU.subtract).then_inc(S["sa_outlo"], 1)

            def evac_res(i, j, s):
                dve.wait_ge(S["slab"], s + 1)
                n = 2 * i + j
                for ps, off, w in bank_parts(j):
                    x = like(XT[:, ds(n * TOK + off, w)], w)
                    ins = nc.vector.tensor_tensor(x, x, ps, ALU.add)
                ins.then_inc(S[f"free{j}"], 1)

            dve.wait_ge(S["pv"], 64)
            start("oA")
            pad()
            t_phase("oA", evac_res)
            rstd(1)
            norm_tiles(1, 1)
            dve.wait_ge(S["rows_out"], 48)

            def ffn(l):
                for c, nf in enumerate(FCH):
                    h0, fill0 = PLAN_H[l][c], PLAN.groups[f"gu{l}{c}"]

                    def evac_gu(i, j, s, h0=h0, fill0=fill0):
                        if j == 0:
                            return
                        dve.wait_ge(S["slab"], s + 1)
                        dve.wait_ge(S["free0"], fill0 + i + 1)
                        dve.wait_ge(S["hx"], h0 + i)
                        for n, (ps, off, w) in enumerate(bank_parts(1)):
                            ins = nc.vector.tensor_tensor(like(HT[:, off:off + w], w), like(GT[:, off:off + w], w), ps, ALU.mult)
                        ins.then_inc(S["free1"], 1)
                        dve.wait_ge(S["hh"], h0 + i)
                        nc.vector.tensor_tensor(HL[:, ds(i * TOK, TOK)], HT[:], HH[:, ds(i * TOK, TOK)].bitcast(F32),
                                                ALU.subtract).then_inc(S["hx"], 1)
                    t_phase(f"gu{l}{c}", evac_gu)
                    if c == len(FCH) - 1:
                        pad()
                    t_phase(f"dn{l}{c}", evac_res)
            dve.sem_inc(S["hx"], 1)
            ffn(0)
            rstd(2)
            norm_tiles(2, 2)

            t_phase("kB", evac_rows(KB, KNB))
            for q in range(2):
                v_phase(dve, PLAN.first["vB"] + 2 * q, 1 + q, lambda m: VST[:, m, 256 * q:256 * q + 256], False)
                for j in range(2):
                    split_lo(PLAN.first["vB"] + 2 * q + 2 + j, j, KT)
            dve.wait_ge(S["vev_act"], 15)
            nc.vector.tensor_copy(VNB[:], VST[:, 8, :]).then_inc(S["vnew"], 1)
            norm_tiles(3, 3)

            def evac_qB(i, j, s, g):
                if j == 1:
                    dve.wait_ge(S["slab"], s + 1)
                    store_q(nc.vector.tensor_copy, 4 * g + 2 * i + 1, 1, PATTERNS[g][1], S["free1"])
            dve.wait_ge(S["vst_out"], 32)
            q_groups(dve, split_lo, evac_qB, PLAN)

            def norm_b(g):
                def norm(b, h):
                    n = 4 * g + b
                    dve.wait_ge(S["pv"], 64 + 32 * g + 8 * b + 4 * h + 4)
                    if not (isinstance(b, int) and n == 0):
                        k = 16 * (n if g < 2 else 8 + 2 * (n - 8))
                        dve.wait_ge(S[f"ust{h}"], k)
                    nc.vector.tensor_copy(UST[h][:, 512:520], SM[:, 8 * h:8 * h + 8])
                    nc.vector.tensor_copy(UST[h][:, 520:528], SM[:, 16 + 8 * h:24 + 8 * h])
                    nc.vector.tensor_copy(UST[h][:, 0:512], PS[:, 4 + h, :]).then_inc(S[f"onorm{h}"], 1)
                return norm
            dve.wait_ge(S["slab"], PLAN.end("qB"))
            for g in range(NG):
                tab = TAB[g]
                full = 256 if g < 2 else P
                attention(64 + 32 * g, 4, 0, widths_b(g),
                          lambda u, kk, w: tab[:, 2 * (u % 4) + kk, full - w:full],
                          ("tab1", "tab4", "tab16")[g], lambda h: 1e38, norm_b(g), None)

            dve.wait_ge(S["tsb"], 32)

            def sample(b, j):
                nc.vector.tensor_copy(TSN[:], TSW[:, :, ds(56 - 8 * b, NEW)]).then_inc(S["sb_tab"], 1)
                dve.wait_ge(S["sb_tab"], b + 1)
                dve.wait_ge(S["sb_s"], b + 1)
                segs = ((3, 0, R16, TSB[:, 0:512], 0), (4, 0, R4, TSB[:, 512:1024], 512), (1, 0, R1, TSB[:, 1024:1152], 1024))
                dve.sem_inc(S["turn"], 1)
                n = 0
                for bank, c0, w, tab, off in segs:
                    nc.vector.tensor_tensor_reduce(out=PSB[:, j, off:off + w], in0=PS[:, bank, c0:c0 + w], in1=tab,
                                                   scale=-SCALE, scalar=1e38 if n == 0 else SM[:, n - 1:n], op0=ALU.add,
                                                   op1=ALU.min, accum_out=SM[:, n:n + 1]).then_inc(S["sb_ttr"], 1)
                    n += 1
                    dve.wait_ge(S["sb_ttr"], 4 * b + n)
                    dve.sem_inc(S["turn"], 1)
                nc.vector.tensor_tensor_reduce(out=PSB[:, j, 1152:SCOLS].rearrange("p (g n) -> p g n", g=NG),
                                               in0=PS[:, 1, P:P + NG * NEW].rearrange("p (g n) -> p g n", g=NG),
                                               in1=TSN[:], scale=-SCALE, scalar=SM[:, 2:3],
                                               op0=ALU.add, op1=ALU.min, accum_out=SM[:, 3:4]).then_inc(S["sb_ttr"], 1)

            def weights(b, j):
                m = MG[j]
                dve.wait_ge(S[f"mg{j}"], 16 * ((b - j + 2) // 2) if not isinstance(b, int) else 16 * (b // 2 + 1))
                nc.vector.tensor_tensor(SM[:, 16:24], m[:, 0, 512:520], m[:, 1, 512:520], ALU.min).then_inc(S["m_min"], 1)
                dve.wait_ge(S["m_min"], 2 * b + 1)
                nc.vector.tensor_tensor(SM[:, 24:32], SM[:, 16:24], m[:, 2, 512:520], ALU.min).then_inc(S["m_min"], 1)
                dve.wait_ge(S["m_min"], 2 * b + 2)
                nc.vector.tensor_tensor(SM[:, 40:64].rearrange("p (g h) -> p g h", g=NG),
                                        SM[:, 24:32].unsqueeze(1).to_broadcast([P, NG, 8]), m[:, :, 512:520],
                                        ALU.subtract).then_inc(S["m_d"], 1)
                dve.wait_ge(S["m_w"], b + 1)
                nc.vector.tensor_tensor(SM[:, 16:40].rearrange("p (g h) -> p g h", g=NG),
                                        SM[:, 40:64].rearrange("p (g h) -> p g h", g=NG), m[:, :, 520:528],
                                        ALU.mult).then_inc(S["m_sum"], 1)
                dve.wait_ge(S["m_sum"], 3 * b + 1)
                nc.vector.tensor_reduce(SM[:, 88:96], SM[:, 16:40].rearrange("p (g h) -> p h g", g=NG),
                                        mybir.AxisListType.X, ALU.add).then_inc(S["m_sum"], 1)
                dve.wait_ge(S["m_sum"], 3 * b + 2)
                nc.vector.reciprocal(SM[:, 16:24], SM[:, 88:96]).then_inc(S["m_sum"], 1)
                dve.wait_ge(S["m_sum"], 3 * b + 3)
                if not (isinstance(b, int) and b == 0):
                    dve.wait_ge(S["m_om"], b)
                nc.vector.tensor_tensor(SM[:, 64:88].rearrange("p (g h) -> p g h", g=NG),
                                        SM[:, 40:64].rearrange("p (g h) -> p g h", g=NG),
                                        SM[:, 16:24].unsqueeze(1).to_broadcast([P, NG, 8]), ALU.mult).then_inc(S["m_c"], 1)

            def sums(b, j):
                q = PSB[:, j, :]
                dve.wait_ge(S["sb_exp"], b + 1)
                if not (isinstance(b, int) and b == 0):
                    dve.wait_ge(S["sb_tr"], 2 * b)
                nc.vector.reciprocal(SM[:, 9:10], SM[:, 8:9]).then_inc(S["sb_p"], 1)
                nc.vector.tensor_tensor(q[:, 512:768], q[:, 512:768], q[:, 256:512], ALU.add).then_inc(S["sb_p"], 1)
                nc.vector.tensor_tensor(q[:, 1152:1216], q[:, 1152:1216], q[:, 1216:1280], ALU.add).then_inc(S["sb_p"], 1)
                dve.wait_ge(S["sb_p"], 6 * b + 3)
                r1 = q[:, 512:1024].rearrange("p (c n) -> p c n", c=2)[:, :, 192:256]
                nc.vector.tensor_tensor(r1, r1, q[:, 1024:1152].rearrange("p (c n) -> p c n", c=2), ALU.add).then_inc(S["sb_p"], 1)
                nc.vector.tensor_tensor(q[:, 1152:1216], q[:, 1152:1216], q[:, 1280:1344], ALU.add).then_inc(S["sb_p"], 1)
                dve.wait_ge(S["sb_p"], 6 * b + 5)
                rl = SM[:, 9:10]
                nc.vector.tensor_scalar(PNB[:, 0:256], q[:, 0:256], rl, None, ALU.mult)
                nc.vector.tensor_scalar(PNB[:, 256:768], q[:, 512:1024], rl, None, ALU.mult)
                nc.vector.tensor_scalar(PNB[:, 768:832], q[:, 1152:1216], rl, None, ALU.mult).then_inc(S["sb_p"], 1)

            def sample_out(b):
                dve.wait_ge(S["sb_tr"], 2 * b + 2)
                if not (isinstance(b, int) and b == 0):
                    dve.wait_ge(S["sb_pv"], b)
                nc.vector.tensor_copy(PTS[:, 4:6, :], PS[:, 6, 0:256].rearrange("p (c n) -> p c n", c=2)).then_inc(S["sb_evD"], 1)
                nc.vector.tensor_copy(PTS[0:64, 6, :], PS[0:64, 6, 256:384]).then_inc(S["sb_evD"], 1)
                for kk in range(2):
                    dve.wait_ge(S["sb_oh"], 2 * b + kk + 1)
                    src = PS[64 * kk:64 * kk + 64, 7, 0:128].rearrange("p (a n) -> p a n", a=4)[:, :, 8 * kk:8 * kk + 8]
                    hi, lo = (XH[64 * kk:64 * kk + 64, z * TOK:(z + 4) * TOK].rearrange("p (k n) -> p k n", k=4)[:, :, ds(SEQ + b * NEWT, NEWT)]
                              for z in (0, 4))
                    nc.vector.tensor_tensor(lo, src, hi.bitcast(F32), ALU.subtract).then_inc(S["sb_ol"], 1)

            def merge_out(b):
                dve.wait_ge(S["m_hi"], b + 1)
                hi, lo = (XH[:, z * TOK:(z + 4) * TOK].rearrange("p (k n) -> p k n", k=4)[:, :, ds(b * P, P)] for z in (0, 4))
                nc.vector.tensor_tensor(lo, PS[:, 0, :].rearrange("p (k n) -> p k n", k=4), hi.bitcast(F32),
                                        ALU.subtract).then_inc(S["m_lo"], 1)

            def batch(b, j, first=False, last=False):
                if not last:
                    weights(b, j)
                    sample(b, j)
                if not first:
                    sample_out(b - 1)
                    merge_out(b - 1)
                if not last:
                    sums(b, j)
            batch(0, 0, first=True)
            batch(1, 1)

            def pair(i):
                batch(2 * i, 0)
                batch(2 * i + 1, 1)
            loop(dve, 1, 4, pair)
            batch(8, 0, last=True)

            start("oB")
            dve.wait_ge(S["rows_out"], 80)
            pad()
            t_phase("oB", evac_res)
            rstd(3)
            norm_tiles(4, 4)
            ffn(1)
            rstd(4)
            norm_tiles(5, 5, final=True)

        @block.tensor
        def _(pe):
            mm = nc.tensor.matmul

            def tiles(x, first=0):
                return lambda k, a, n: x[:, (k + first) * TOK + a:(k + first) * TOK + a + n]

            def slab(s, j, nk, hi, lo, fill, operand):
                pe.wait_ge(S["wl"], s + 1)
                if not (isinstance(fill, int) and fill == 0):
                    pe.wait_ge(S[f"free{j}"], fill)
                for k in range(nk):
                    if operand:
                        operand(k)
                    for n, (w, x) in enumerate(((WH, hi), (WH, lo), (WL, hi))):
                        for c, (a, width) in enumerate(CH):
                            ins = mm(PS[:, 3 * j + c, 0:width], w[:, j, k * P:(k + 1) * P], x(k, a, width),
                                     start=(k == 0 and n == 0), stop=(k == nk - 1 and n == 2))
                ins.then_inc(S["slab"], 1)

            def t_phase(name, hi, lo, operand, norm=None):
                s0, n, nk, g0 = PLAN.first[name], PLAN.count[name], PLAN.depth[name], PLAN.groups[name]

                def pair(i, first=False):
                    for j in range(2):
                        slab(s0 + 2 * i + j, j, nk, hi, lo, g0 + i, operand)
                        if norm is not None and not first:
                            ssq(norm, 2 * i - 2 + j, j)
                if norm is None:
                    loop(pe, 0, n // 2, pair)
                else:
                    pair(0, True)
                    pair(1)
                    loop(pe, 2, n // 2, pair)
                    ssq(norm, n - 2, 0)
                    ssq(norm, n - 1, 1)

            def ssq(norm, k, j):
                pe.wait_ge(S["sq"], KT * norm + k + 1)
                first, last = (isinstance(k, int) and k == x for x in (0, KT - 1))
                for m in range(MT):
                    ins = mm(PS[:, 6, m:m + 1], SQ[:, j, m * P:(m + 1) * P], ONES[:, 0:1], start=first and m == 0,
                             stop=last, skip_group_check=True)
                ins.then_inc(S["ssq"], 1)

            def spread(norm, after):
                pe.wait_ge(S["diag"], norm + 1)
                if after:
                    groups_done(pe, after)
                for m in range(MT):
                    w = min(P, TOK - m * P)
                    ins = mm(PS[:, 3 + m // 3, (m % 3) * P:(m % 3) * P + w], ONES[:], DIAG[:, m, 0:w], start=True, stop=True)
                ins.then_inc(S["rbc"], 1)

            def v_phase(s, which, after):
                groups_done(pe, after)
                pe.wait_ge(S["wl"], s + 2)
                for m in range(MT):
                    if m < 6 and which:
                        pe.wait_ge(S["vev_act"], 5 * which)
                        pe.wait_ge(S["vev_dve"], 4 * which)
                    if m >= 6:
                        pe.wait_ge(S["vev_dve" if m % 2 else "vev_act"], (4 if m % 2 else 5) * which + (m - 6) // 2 + 1)
                    for k in range(KT):
                        for n, (w, x) in enumerate(((WH, XH), (WH, XL), (WL, XH))):
                            ins = mm(PS[:, m % 6, 0:256].rearrange("p (a n) -> p a n", a=2),
                                     x[:, k * TOK + m * P:k * TOK + (m + 1) * P], w[:, :, k * P:(k + 1) * P],
                                     start=(k == 0 and n == 0), stop=(k == KT - 1 and n == 2))
                    if m == MT - 1:
                        ins.then_inc(S["slab"], 2)
                    else:
                        ins.then_inc(S["vps"], 1)

            def v_read(which):
                pe.wait_ge(S["vev_act"], 5 * which)
                pe.wait_ge(S["vev_dve"], 4 * which)

            def xn_ready(x):
                return lambda k: pe.wait_ge(S["xn"], KT * x + k + 1)
            XHT, XLT = tiles(XH), tiles(XL)

            pe.wait_ge(S["ones"], 1)
            pe.wait_ge(S["pad"], 1)
            for k in range(KT):
                ssq(0, k, k % 2)
            spread(0, None)
            t_phase("kA", XHT, XLT, xn_ready(0))
            v_phase(PLAN.first["vA"], 0, "kA")
            v_read(1)
            t_phase("qA", XHT, XLT, None)

            def attention(units0, n_bodies, peel, widths, keys, values, finish):
                def scores(i, u, w, first):
                    U = units0 + 8 * i + u
                    pe.wait_ge(S["stage"], U + 1)
                    if not (isinstance(U, int) and U < 2):
                        pe.wait_ge(S["ttr"], U - 1)
                    for kk in range(2):
                        ins = mm(PS[:, u % 2, kk * w:(kk + 1) * w], STG[:, 2 * u + kk, :], keys(i, u, w, first),
                                 start=True, stop=True)
                    ins.then_inc(S["score"], 1)

                def transposes(i, u, w):
                    U = units0 + 8 * i + u
                    pe.wait_ge(S["exp"], U + 1)
                    if not (isinstance(U, int) and U < 2):
                        pe.wait_ge(S[f"pev{u % 2}"], units0 // 2 + 4 * i + u // 2)
                    for kk in range(2):
                        for c in range(w // P):
                            ins = nc.tensor.transpose(PS[:, 2 + u % 2, kk * w + c * P:kk * w + (c + 1) * P],
                                                      SB[:, u % 4, kk, c * P:(c + 1) * P], IDN[:])
                    ins.then_inc(S["tr"], 1)

                def pv(i, u, w, first):
                    pe.wait_ge(S[f"pev{u % 2}"], units0 // 2 + 4 * i + u // 2 + 1)
                    if u % 4 == 0 and not (isinstance(i, int) and units0 + i == 0):
                        pe.wait_ge(S[f"onorm{u // 4}"], units0 // 8 + i)
                    for kk in range(2):
                        o = (2 * (u % 4) + kk) * HD
                        for c in range(w // P):
                            ins = mm(PS[:, 4 + u // 4, o:o + HD], PT[:, u % 2, kk * w + c * P:kk * w + (c + 1) * P],
                                     values(i, u, kk, c, w, first), start=(c == 0), stop=(c == w // P - 1))
                    ins.then_inc(S["pv"], 1)

                def body(i, prev, cur=True, first=False, prev_first=False):
                    for st in range(8):
                        if cur:
                            scores(i, st, widths(st, first), first)
                        for lag, what in ((2, transposes), (3, pv)):
                            v = (st - lag) % 8
                            own = st >= lag
                            if own and not cur or not own and prev is None:
                                continue
                            b, f = (i, first) if own else (prev, prev_first)
                            if what is pv:
                                pv(b, v, widths(v, f), f)
                            else:
                                transposes(b, v, widths(v, f))
                        if finish:
                            finish(i, prev, st, cur)
                body(0, None, first=True)
                if peel:
                    body(1, 0, prev_first=True)
                loop(pe, 1 + peel, n_bodies, lambda i: body(i, i - 1))
                body(n_bodies, n_bodies - 1, cur=False)

            def finish_a(i, prev, st, cur):
                def otr(b, h):
                    pe.wait_ge(S[f"onorm{h}"], b + 1)
                    if not (isinstance(b, int) and b == 0):
                        pe.wait_ge(S["olo"], 2 * b + h - 1)
                    for c in range(4):
                        ins = nc.tensor.transpose(PS[:, 6 + h, c * P:(c + 1) * P], OSB[:, h, c * P:(c + 1) * P], IDN[:])
                    ins.then_inc(S["otr"], 1)
                if st == 7 and cur:
                    otr(i, 0)
                if st == 3 and prev is not None:
                    otr(prev, 1)

            def keys_a(i, u, w, first):
                a = u // 4
                return KA[:, ds(a * TOK + (0 if first else (i - 1) * P), w)]

            def values_a(i, u, kk, c, w, first):
                a = u // 4
                m = 0 if first else i - 1 + c
                d = (2 * a + kk) * HD
                return VA[:, ds(m, 1), d:d + HD].rearrange("p m d -> p (m d)")

            groups_done(pe, "qA")
            attention(0, 8, 1, lambda u, first: P if first else 256, keys_a, values_a, finish_a)

            pe.wait_ge(S["cA"], 48)
            pe.wait_ge(S["sa_q"], 2)
            for b in range(NEWB):
                if b >= 2:
                    pe.wait_ge(S["sa_ttr"], 2 * b - 2)
                for a in range(2):
                    for kk in range(2):
                        r, o = slice(64 * kk, 64 * kk + 64), 32 * (2 * a + kk)
                        q = QNS[r, a, b, :]
                        mm(PS[o:o + 32, b % 2, 0:P], q, KCA[r, b, a, :], start=True, stop=True)
                        ins = mm(PS[o:o + 32, b % 2, P:192], q, KA[r, a * TOK + SEQ:(a + 1) * TOK], start=True, stop=True)
                ins.then_inc(S["sa_s"], 1)
            pe.wait_ge(S["sa_p"], 3)
            for q in range(2):
                for b in range(4):
                    ins = nc.tensor.transpose(PS[:, 2 + q, b * P:(b + 1) * P], PSA[:, 4 * q + b, 0:P], IDN[:])
                ins.then_inc(S["sa_tr"], 1)
            for q in range(2):
                for b in range(4):
                    ins = nc.tensor.transpose(PS[0:64, 4 + q, b * P:(b + 1) * P], PSA[:, 4 * q + b, P:192], IDN[:])
                ins.then_inc(S["sa_tr"], 1)
            pe.wait_ge(S["sa_evA"], 2)
            pe.wait_ge(S["sa_evD"], 2)
            pe.wait_ge(S["olo"], 16)
            for a in range(2):
                for b in range(NEWB):
                    o = PS[:, 6 + a, b * 64:(b + 1) * 64]
                    mm(o, VCA[:, b, a * P:(a + 1) * P], PTA[:, b, a * 64:(a + 1) * 64], start=True, stop=False)
                    ins = mm(o, VA[0:NEW, 8, a * P:(a + 1) * P], PTN[0:NEW, b, a * 64:(a + 1) * 64], start=False, stop=True)
                ins.then_inc(S["sa_pv"], 1)

            pe.wait_ge(S["sa_outlo"], 4)
            pe.wait_ge(S["pad"], 2)
            t_phase("oA", XHT, XLT, None, norm=1)
            spread(1, "oA")

            def ffn(l, x):
                for c, nf in enumerate(FCH):
                    h0 = PLAN_H[l][c]
                    t_phase(f"gu{l}{c}", XHT, XLT, xn_ready(x) if c == 0 else None)
                    last = c == len(FCH) - 1
                    if last:
                        pe.wait_ge(S["pad"], 3 + 2 * l)
                    t_phase(f"dn{l}{c}", tiles(HH), tiles(HL), lambda k: pe.wait_ge(S["hx"], h0 + k + 1),
                            norm=2 + 2 * l if last else None)
                spread(2 + 2 * l, f"dn{l}{len(FCH) - 1}")
            ffn(0, 1)

            t_phase("kB", XHT, XLT, xn_ready(2))
            for q in range(2):
                v_phase(PLAN.first["vB"] + 2 * q, 1 + q, "kB")
            v_read(3)
            spread(2, "kB")
            t_phase("qB", XHT, XLT, xn_ready(3))
            groups_done(pe, "qB")

            def keys_b(g):
                src = KB if g == 0 else KP[g - 1]

                def keys(i, u, w, first):
                    p, h = u % 4, u // 4
                    if g == 0:
                        off = 0 if first and h == 0 else (2 * i - 1 + h) * P
                    elif g == 1:
                        off = 2 * i * P
                    else:
                        off = (2 * i + h) * P
                    return src[:, ds(p * SEQ + off, w)]
                return keys

            def values_b(g):
                def values(i, u, kk, c, w, first):
                    p, h = u % 4, u // 4
                    if g == 0:
                        m = 0 if first and h == 0 else 2 * i - 1 + h + c
                    elif g == 1:
                        m = 2 * i + c
                    else:
                        m = 2 * i + h
                    d = (2 * p + kk) * HD
                    return VG[g % 2][:, ds(m, 1), d:d + HD].rearrange("p m d -> p (m d)")
                return values
            for g in range(NG):
                pe.wait_ge(S[f"vg{g % 2}"], (16, 64, 48)[g])
                if g:
                    pe.wait_ge(S["kperm"], 4 * g)
                attention(64 + 32 * g, 4, 0, widths_b(g), keys_b(g), values_b(g), None)

            def sample_scores(b, j):
                pe.wait_ge(S["sb_stage"], 2 * b + 2)
                pe.wait_ge(S[f"kc{j}"], 16 * raw_count(b, j))
                if not (isinstance(b, int) and b == 0):
                    pe.wait_ge(S["sb_ttr"], 4 * b)
                for p in range(4):
                    o = slice(32 * p, 32 * p + 32)
                    mm(PS[o, 3, 0:512], SQN[:, 2, p, :], KC[:, j, p, 0:512], start=True, stop=True)
                    mm(PS[o, 4, 0:512], SQN[:, 1, p, :], KC[:, j, p, 256:768], start=True, stop=True)
                    k1 = KC[:, j, p, 256:768].rearrange("p (c n) -> p c n", c=2)[:, :, 192:256]
                    mm(PS[o, 1, 0:P].rearrange("p (c n) -> p c n", c=2), SQN[:, 0, p, :], k1, start=True, stop=True)
                    for g in range(NG):
                        c0 = P + g * NEW
                        ins = mm(PS[o, 1, c0:c0 + NEW], SQN[:, g, p, :], KNB[:, p, :], start=True, stop=True)
                ins.then_inc(S["sb_s"], 1)

            def sample_values(b, j):
                pe.wait_ge(S["sb_p"], 6 * b + 6)
                if not (isinstance(b, int) and b == 0):
                    pe.wait_ge(S["sb_evA"], b)
                    pe.wait_ge(S["sb_evD"], 2 * b)
                for c in range(4):
                    ins = nc.tensor.transpose(PS[:, 5, c * P:(c + 1) * P], PNB[:, c * P:(c + 1) * P], IDN[:])
                ins.then_inc(S["sb_tr"], 1)
                for c in range(2):
                    nc.tensor.transpose(PS[:, 6, c * P:(c + 1) * P], PNB[:, (4 + c) * P:(5 + c) * P], IDN[:])
                nc.tensor.transpose(PS[0:NEW, 6, 256:384], PNB[:, KEPT:KEPT + NEW], IDN[:]).then_inc(S["sb_tr"], 1)
                pe.wait_ge(S["sb_evA"], b + 1)
                pe.wait_ge(S["sb_evD"], 2 * b + 2)
                pe.wait_ge(S[f"vc{j}"], 16 * raw_count(b, j))
                if not (isinstance(b, int) and b == 0):
                    pe.wait_ge(S["sb_ol"], 2 * b)
                for p in range(4):
                    o = PS[:, 7, 32 * p:32 * p + 32]
                    for c in range(6):
                        mm(o, VC[:, j, c, p * P:(p + 1) * P], PTS[:, c, 32 * p:32 * p + 32], start=(c == 0), stop=False)
                    ins = mm(o, VNB[0:NEW, p * P:(p + 1) * P], PTS[0:NEW, 6, 32 * p:32 * p + 32], start=False, stop=True)
                ins.then_inc(S["sb_pv"], 1)
                pe.wait_ge(S["m_om"], b + 1)
                if not (isinstance(b, int) and b == 0):
                    pe.wait_ge(S["m_lo"], b)
                for c in range(4):
                    ins = nc.tensor.transpose(PS[:, 0, c * P:(c + 1) * P], OM[:, c * P:(c + 1) * P], IDN[:])
                ins.then_inc(S["m_tr"], 1)

            pe.wait_ge(S["onorm0"], 8 + 12)
            pe.wait_ge(S["onorm1"], 8 + 12)
            sample_scores(0, 0)
            sample_scores(1, 1)
            sample_values(0, 0)

            def pair(i):
                sample_scores(2 * i, 0)
                sample_values(2 * i - 1, 1)
                sample_scores(2 * i + 1, 1)
                sample_values(2 * i, 0)
            loop(pe, 1, 4, pair)
            sample_values(7, 1)

            pe.wait_ge(S["sb_ol"], 16)
            pe.wait_ge(S["m_lo"], 8)
            pe.wait_ge(S["pad"], 4)
            t_phase("oB", tiles(XH), tiles(XH, 4), None, norm=3)
            spread(3, "oB")
            ffn(1, 4)


def slopes(n):
    return np.asarray(2.0 ** (-8.0 * (np.arange(n) + 1) / n), dtype=np.float32)


def penalty(slope, dist, valid):
    d = -(np.float32(slope) * dist.astype(np.float32)) * np.float32(UNSCALE)
    return np.where(valid, d, np.float32(NEG)).astype(np.float32)


def key_order():
    k = np.arange(PAST)
    low, near = k % 16 < 8, k >= PAST // 2
    return np.concatenate([k[low & ~near], k[low & near], k[~low & near], k[~low & ~near]])


def a_head(u, kk):
    return A_GRP * (2 * (u // A_GRP) + kk) + u % A_GRP


def host_tables():
    sa, sb = slopes(A_HEADS), slopes(NG * B_SLOTS).reshape(NG, B_SLOTS)
    q, k = np.arange(P)[:, None], np.arange(256)[None, :]
    d = P + q - k
    t = {}
    order = [a_head(u, kk) for u in range(8) for kk in range(2)]
    t["tabA"] = np.stack([penalty(sa[h], d, (d >= 0) & (d < P)) for h in order], 1)
    for g, name in ((0, "tabB1"), (1, "tabB4")):
        r = PATTERNS[g][1]
        t[name] = np.stack([penalty(sb[g, h], r * d, (d >= 0) & (d <= P)) for h in range(B_SLOTS)], 1)
    d = q - np.arange(P)[None, :]
    same = (q // 64) == (np.arange(P)[None, :] // 64)
    t["tabB16"] = np.stack([penalty(sb[2, h], 16 * d, (d >= 0) & same) for h in range(B_SLOTS)], 1)
    row = np.arange(P)
    i = row % 8
    sl = sa[row // 8][:, None]
    dc = P + i[:, None] - np.arange(P)[None, :]
    w = np.arange(120)[None, :] - 56
    dn = i[:, None] - w
    new = (w >= 0) & (w < 8) & (dn >= 0)
    t["tabSA"] = np.concatenate([penalty(sl, dc, (dc >= 0) & (dc < P)), penalty(sl, dn, new)], 1)
    used = (row % 32 < 16)[:, None]
    head = 2 * (row // 32) + (row % 32 // 8) % 2
    pos = PAST + i[:, None]
    ko = key_order()
    seg = []
    for g, keys in ((2, ko[0:512]), (1, ko[256:768]), (0, np.concatenate([ko[448:512], ko[704:768]]))):
        wdw, r = PATTERNS[g]
        dist = pos - keys[None, :]
        ok = (dist >= 0) & (dist <= wdw) & (dist % r == 0)
        seg.append(np.where(used, penalty(sb[g, head][:, None], dist, ok), 0))
    t["tabSB"] = np.concatenate(seg, 1).astype(np.float32)
    t["tabSW"] = np.stack([np.where(used, penalty(sb[g, head][:, None], dn, new & (dn % PATTERNS[g][1] == 0)), 0)
                           for g in range(NG)], 1).astype(np.float32)
    t["ident"] = np.eye(P, dtype=np.float32)
    return t


def slab_layout(w, cols):
    k = w.shape[0] // P
    return np.ascontiguousarray(w.reshape(k, P, -1)[:, :, cols].transpose(2, 1, 0, 3).reshape(len(cols), P, k * P))


def kernel(**inputs):
    import concourse.bacc as bacc
    from concourse.bass_utils import run_bass_kernel_spmd

    x = {n: np.asarray(a) for n, a in inputs.items()}
    feed = host_tables()
    cont = np.ascontiguousarray
    tokens = np.concatenate([x["x_prompt"].reshape(SEQ, DM), x["x_sample"].reshape(NEW, DM)], 0)
    feed["xT"] = cont(tokens.T.reshape(KT, P, TOK))
    gains = np.stack([x["g_attn"][0], x["g_ffn"][0], x["g_kv"], x["g_attn"][1], x["g_ffn"][1], x["g_final"]])
    feed["gains"] = cont(gains.reshape(6, KT, P).transpose(2, 0, 1).reshape(P, 6 * KT))
    sinks = x["sinks_a"][0]
    order = [a_head(u, kk) for u in range(8) for kk in range(2)]
    feed["sinks"] = cont(np.broadcast_to(sinks[order], (P, 16)))
    feed["sinkS"] = cont(np.repeat(sinks, 8)[:, None])
    tile = lambda n0, n: n0 + np.arange(n * P).reshape(n, P)
    wa = x["w_qkv_a"][0]
    hcol = np.array([[a_head(u, kk) * HD + d for kk in range(2) for d in range(HD)] for u in range(8)])
    feed["w_kA"], feed["w_vA"] = slab_layout(wa, tile(1024, 2)), slab_layout(wa, tile(1280, 2))
    feed["w_qA"] = slab_layout(wa, hcol)
    feed["w_oA"] = slab_layout(x["w_o_a"][0][hcol.reshape(-1)], tile(0, 8))
    feed["w_kB"], feed["w_vB"] = slab_layout(x["w_kv_s"], tile(0, 4)), slab_layout(x["w_kv_s"], tile(512, 4))
    feed["w_qB"] = slab_layout(x["w_q_b"][0], tile(0, 12))
    feed["w_oB"] = slab_layout(x["w_o_b"][0], tile(0, 8))
    for l in range(2):
        gu, dn = x["w_gate_up"][l], x["w_down"][l]
        f0 = 0
        for c, n in enumerate(FCH):
            cols = np.stack([tile(f0 * P, n), tile(DFF + f0 * P, n)], 1).reshape(2 * n, P)
            feed[f"w_gu{l}{c}"] = slab_layout(gu, cols)
            feed[f"w_dn{l}{c}"] = slab_layout(dn[f0 * P:(f0 + n) * P], tile(0, 8))
            f0 += n
    ko = key_order()
    feed["ak_in"] = cont(x["cache_a_k"][0].reshape(NEWB, P, 256).transpose(0, 2, 1))
    feed["av_in"] = cont(x["cache_a_v"][0].reshape(NEWB, P, 256))
    feed["bk_in"] = cont(x["cache_b_k"].reshape(NEWB, PAST, 512)[:, ko].transpose(0, 2, 1))
    feed["bv_in"] = cont(x["cache_b_v"].reshape(NEWB, PAST, 512)[:, ko])
    outs = {"yT": (KT, P, TOK), "akT": (P, 2, P + NEW), "avN": (P + NEW, 256), "akS": (NEWB, 256, P - NEWT),
            "avS": (NEWB, P - NEWT, 256), "bkT": (P, 4 * SEQ), "bkN": (P, 4, NEW), "bv": (TOK, 512),
            "bkS": (NEWB, 512, PAST - NEWT), "bvS": (NEWB, PAST - NEWT, 512)}

    nc = bacc.Bacc("TRN2", target_bir_lowering=False, num_devices=1)
    t = {n: nc.dram_tensor(f"in_{n}", a.shape, F32, kind="ExternalInput").ap() for n, a in feed.items()}
    t |= {n: nc.dram_tensor(f"out_{n}", s, F32, kind="ExternalOutput").ap() for n, s in outs.items()}
    t["u"] = nc.dram_tensor("u", (NG, SEQ, UROW), F32, kind="Internal").ap()
    program(nc, t)
    got = run_bass_kernel_spmd(nc, [{f"in_{n}": a for n, a in feed.items()}], core_ids=[0]).results[0]
    r = {n: np.asarray(got[f"out_{n}"]) for n in outs}

    y = r["yT"].reshape(DM, TOK).T
    ak = r["akT"].transpose(2, 1, 0).reshape(P + NEW, A_KV, HD)
    av = r["avN"].reshape(P + NEW, A_KV, HD)
    bkp = r["bkT"].reshape(P, 4, SEQ).transpose(2, 1, 0).reshape(SEQ, B_SLOTS, HD)
    bkn = r["bkN"].transpose(2, 1, 0).reshape(NEWB, NEWT, B_SLOTS, HD)
    bvp = r["bv"][:SEQ].reshape(SEQ, B_SLOTS, HD)
    bvn = r["bv"][SEQ:].reshape(NEWB, NEWT, B_SLOTS, HD)
    back = np.argsort(ko[NEWT:])
    bks = r["bkS"].transpose(0, 2, 1)[:, back].reshape(NEWB, PAST - NEWT, B_SLOTS, HD)
    bvs = r["bvS"][:, back].reshape(NEWB, PAST - NEWT, B_SLOTS, HD)
    aks = r["akS"].transpose(0, 2, 1).reshape(NEWB, P - NEWT, A_KV, HD)
    avs = r["avS"].reshape(NEWB, P - NEWT, A_KV, HD)
    new = lambda z: z[P:].reshape(NEWB, NEWT, A_KV, HD)
    return (cont(y[:SEQ].reshape(1, SEQ, DM)), cont(y[SEQ:].reshape(NEWB, NEWT, DM)),
            cont(ak[:P][None, None]), cont(av[:P][None, None]), cont(bkp[None]), cont(bvp[None]),
            cont(np.concatenate([aks, new(ak)], 1)[None]), cont(np.concatenate([avs, new(av)], 1)[None]),
            cont(np.concatenate([bks, bkn], 1)), cont(np.concatenate([bvs, bvn], 1)))
```

```python
import numpy as np

import concourse.bass as bass
from concourse import mybir
from concourse.alu_op_type import AluOpType as ALU

F32 = mybir.dt.float32
F32R = mybir.dt.float32r
ACT = mybir.ActivationFunctionType

P = 128
DM = 1024
SEQ = 1024
NEWB, NEWT = 8, 8
NEW = NEWB * NEWT
TOK = SEQ + NEW
KT = DM // P
HD = 64
A_HEADS, A_KV, A_GRP = 16, 4, 4
B_SLOTS = 8
PATTERNS = ((128, 1), (512, 4), (2048, 16))
NG = len(PATTERNS)
DFF = -(-8 * DM // (3 * 256)) * 256
FT = DFF // P
PAST = 1024
EPS = 1e-6
NEG = -1e30
SCALE = HD ** -0.5
UNSCALE = 1.0 / SCALE
CH = ((0, 384), (384, 384), (768, TOK - 768))
MT = -(-TOK // P)
FCH = (6, 6, 5, 5)
UROW = B_SLOTS * HD + 2 * B_SLOTS
KEPT = 768
LAG = 3
PV_LAG = LAG + 2
YPOOL = 2
R16, R4, R1 = 512, 512, 128
SCOLS = R16 + R4 + R1 + NG * NEW


def phases():
    out = [("kA", 2, KT), ("vA", 2, KT), ("qA", 8, KT), ("oA", 8, KT)]
    for l in range(2):
        if l == 1:
            out += [("kB", 4, KT), ("vB", 4, KT), ("qB", 12, KT), ("oB", 8, 4)]
        for c, n in enumerate(FCH):
            out += [(f"gu{l}{c}", 2 * n, KT), (f"dn{l}{c}", 8, n)]
    return out


class Plan:

    def __init__(self):
        self.first, self.groups, self.count, self.depth, self.order = {}, {}, {}, {}, []
        self.scaled = {}
        s = g = z = 0
        for name, n, nk in phases():
            self.first[name], self.groups[name], self.count[name], self.depth[name] = s, g, n, nk
            self.order.append(name)
            s += n
            self.scaled[name] = z
            z += n if name[:2] not in ("oA", "oB", "dn") else 0
            g += 0 if name[0] == "v" else n // 2

    def end(self, name):
        return self.first[name] + self.count[name]

    def next(self, name):
        at = self.order.index(name) + 1
        return self.order[at] if at < len(self.order) else None

    def next_depth(self, name):
        return self.depth.get(self.next(name))


PLAN = Plan()


def program(nc, t):
    from contextlib import ExitStack
    ctx = ExitStack()
    with ctx:
        base = [16512]

        def at(name, shape, off, dt=F32):
            return nc.alloc_sbuf_tensor_at(name, shape, dt, offset=off)

        def take(nbytes):
            off = base[0]
            base[0] += -(-nbytes // 32) * 32
            return off

        W4 = 4 * TOK
        XT = at("XT", [P, KT * TOK], take(KT * W4))
        o_xh, o_xl = take(KT * W4 + 256), take(KT * W4 + 256)
        XH = at("XH", [P, KT * TOK + 64], o_xh, F32R)
        XL = at("XL", [P, KT * TOK + 64], o_xl, F32R)
        o_raw, o_wh, o_wl = take(8192), take(8192), take(8192)
        RAW = at("RAW", [P, 2, KT * P], o_raw)
        WH = at("WH", [P, 2, KT * P], o_wh, F32R)
        WL = at("WL", [P, 2, KT * P], o_wl, F32R)
        IDN = at("IDN", [P, P], take(512))
        ONES = at("ONES", [P, P], take(512))
        GAIN = at("GAIN", [P, 6 * KT], take(4 * 6 * KT))
        SINK = at("SINK", [P, 16], take(64))
        NSINK = at("NSINK", [P, 16], take(64))
        SINKS = at("SINKS", [P, 2], take(8))
        STD = at("STD", [P, MT], take(64))
        RST = at("RST", [P, MT], take(64))
        EPSB = at("EPSB", [P, 1], take(4))
        SM = at("SM", [P, 96], take(384))
        R = base[0]
        assert R + 80000 <= 229344, R
        HH = at("HH", [P, FCH[0] * TOK], R, F32R)
        HL = at("HL", [P, FCH[0] * TOK], R + FCH[0] * W4, F32R)
        GT = at("GT", [P, TOK], R + 52224)
        HT = at("HT", [P, TOK], R + 56576)
        SQ = at("SQ", [P, 2, TOK], R + 60928)
        RB = at("RB", [P, TOK], R + 71680)
        SQS = at("SQS", [P, MT * P], R + 76032)
        YT = at("YT", [P, KT, TOK], R)
        QA = at("QA", [P, 8 * SEQ], R)
        KA = at("KA", [P, 2 * TOK], R + 32768)
        VA = at("VA", [P, MT, 256], R + 41472)
        TABA = at("TABA", [P, 16, 256], R + 50688)
        QNA = at("QNA", [P, 8, NEW], R + 67072)
        QNS = at("QNS", [P, 2, NEWB, 32], R + 69120)
        STG = at("STG", [P, 16, P], R + 71680)
        SB = at("SB", [P, 4, 2, 256], o_wh)
        PT = at("PT", [P, 2, 512], o_wl)
        OSB = at("OSB", [P, 2, 512], o_wl + 4096)
        KCA = at("KCA", [P, NEWB, 2, P], R)
        VCA = at("VCA", [P, NEWB, 256], R + 8192)
        PSA = at("PSA", [P, NEWB, 192], R + 16384)
        PTA = at("PTA", [P, NEWB, P], R + 22528)
        PTN = at("PTN", [P, NEWB, P], R + 26624)
        TSA = at("TSA", [P, P + 120], R + 30720)
        QB = at("QB", [P, 12 * SEQ], R)
        KB = at("KB", [P, 4 * SEQ], R + 49152)
        QNB = at("QNB", [P, 12, NEW], R + 65536)
        KNB = at("KNB", [P, 4, NEW], R + 68608)
        VNB = at("VNB", [P, 512], R + 69632)
        VST = at("VST", [P, MT, 512], R)
        VG = [at("VG0", [P, 8, 512], o_xh), at("VG1", [P, 8, 512], o_xh + 16384)]
        KP = [at("KP4", [P, 4 * SEQ], o_xl), at("KP16", [P, 4 * SEQ], o_xl + 16384)]
        TAB = [at("TAB1", [P, 8, 256], o_raw), at("TAB4", [P, 8, 256], R), at("TAB16", [P, 8, P], R + 8192)]
        UST = [at("UST0", [P, UROW], o_xh + 32768), at("UST1", [P, UROW], o_xl + 32768)]
        KC = at("KC", [P, 2, 4, KEPT], R + 12288)
        VC = at("VC", [P, 2, 6, 512], R + 36864)
        SQN = at("SQN", [P, NG, 4, 32], o_xl)
        TSB = at("TSB", [P, R16 + R4 + R1], o_xl + 1536)
        TSN = at("TSN", [P, NG, NEW], R + 79872)
        TSW = at("TSW", [P, NG, 120], o_xl + 6144)
        PSB = at("PSB", [P, 2, SCOLS], o_xl + 7584)
        PTS = at("PTS", [P, 7, P], o_xl + 18336)
        OM = at("OM", [P, 512], o_xl + 21920)
        OS = at("OS", [P, P], o_xl + 34400)
        PNB = at("PNB", [P, KEPT + NEW], o_xl + 23968)
        MG = [at("MG0", [P, NG, UROW], o_xl + 27296), at("MG1", [P, NG, UROW], R)]
        PS = ctx.enter_context(nc.psum_tensor("PS", [P, 8, 512], F32))

        names = """raw0 raw1 wh wl slab free0 free1 vps vev_act vev_dve const ones gain pad
            sq sqs sums std rb eps xh xn silu gt yg yp yt yout scaled hh hx
            stage clear score ttr exp tr pev0 pev1 pv dsink esink rl stat onorm0 onorm1 otr ohi olo
            tabA nsink tab1 tab4 tab16 kperm vnew vst_out vg0 vg1 ust0 ust1
            cA tsa sa_q sa_s sa_ttr sa_exp sa_es sa_p sa_tr sa_evA sa_evD sa_pv sa_out sa_outlo
            kc0 kc1 vc0 vc1 tsb sb_tab sb_stage sb_zero sb_s sb_ttr sb_exp sb_p sb_tr sb_evA sb_evD sb_pv sb_os sb_otr sb_oh sb_ol
            turn mg0 mg1 m_min m_d m_w m_sum m_c m_add m_om m_tr m_hi m_lo rows_out copies""".split()
        S = {n: ctx.enter_context(nc.semaphore("s_" + n)) for n in names}
        xin = [ctx.enter_context(nc.semaphore(f"s_xin{k}")) for k in range(KT)]
        block = ctx.enter_context(nc.Block())

        ds = bass.ds

        def bank_parts(j):
            return ((PS[:, 3 * j:3 * j + 2, 0:384], 0, 768), (PS[:, 3 * j + 2:3 * j + 3, 0:CH[2][1]], 768, CH[2][1]))

        def like(ap, j_cols):
            return ap.rearrange("p (c n) -> p c n", c=2 if j_cols == 768 else 1)

        def loop(eng, lo, hi, body):
            if hi - lo == 1:
                body(lo)
            elif hi > lo:
                with eng.Fori(lo, hi, 1) as i:
                    body(i)

        def groups_done(eng, name):
            for j in range(2):
                eng.wait_ge(S[f"free{j}"], PLAN.groups[name] + PLAN.count[name] // 2)

        def keys_of(b):
            w = t["bk_in"]
            w = w[b] if isinstance(b, int) else w[ds(b, 1)].rearrange("b f k -> (b f) k")
            return w.rearrange("(c p) k -> p c k", p=P)[:, :, 0:KEPT]

        def values_of(b):
            w = t["bv_in"]
            w = w[b] if isinstance(b, int) else w[ds(b, 1)].rearrange("b k d -> (b k) d")
            return w.rearrange("(c p) d -> p c d", p=P)[:, 0:6]

        def copies(sp, c):
            sp.dma_start(t["bkS"][c], t["bk_in"][c, :, NEWT:PAST]).then_inc(S["copies"], 16)
            sp.dma_start(t["bvS"][c], t["bv_in"][c, NEWT:PAST, :]).then_inc(S["copies"], 16)
            if c == 0:
                sp.dma_start(t["akS"], t["ak_in"][:, :, NEWT:P]).then_inc(S["copies"], 16)
                sp.dma_start(t["avS"], t["av_in"][:, NEWT:P, :]).then_inc(S["copies"], 16)

        def store_u(sp, body0, dst, g, lo=0, hi=4):
            def body(b):
                for h in range(2):
                    sp.wait_ge(S[f"onorm{h}"], 8 + body0 + b + 1)
                    d = dst[b, h] if isinstance(b, int) else dst[ds(b, 1), h]
                    if g == 2:
                        for r in range(2):
                            dd = d[r] if isinstance(b, int) else d[:, r].rearrange("b i d -> (b i) d")
                            sp.dma_start(dd, UST[h][64 * r:64 * r + 64, :]).then_inc(S[f"ust{h}"], 16)
                    else:
                        dd = d if isinstance(b, int) else d.rearrange("b p d -> (b p) d")
                        sp.dma_start(dd, UST[h][:]).then_inc(S[f"ust{h}"], 16)
            loop(sp, lo, hi, body)

        def store_q(n, j, r):
            q = QB[:, n * SEQ:(n + 1) * SEQ].rearrange("p (r i) -> p r i", r=r)
            for c, w in ((0, 384), (1, 384), (2, 256)):
                src = PS[:, 3 * j + c, 0:w].rearrange("p (i r) -> p r i", r=r)
                rb = RB[:, 384 * c:384 * c + w].rearrange("p (i r) -> p r i", r=r)
                nc.vector.tensor_tensor(q[:, :, 384 * c // r:(384 * c + w) // r], src, rb, ALU.mult)
            nc.vector.tensor_tensor(QNB[:, n, :], PS[:, 3 * j + 2, 256:320], RB[:, SEQ:TOK], ALU.mult).then_inc(S[f"free{j}"], 1)

        def widths_b(g):
            if g == 0:
                return lambda u, first: P if first and u < 4 else 256
            if g == 1:
                return lambda u, first: P if u < 4 else 256
            return lambda u, first: P

        def v_phase(eng, s, which, dst, is_act):
            for m in range(0 if is_act else 1, MT, 2):
                if m == MT - 1:
                    eng.wait_ge(S["slab"], s + 2)
                else:
                    eng.wait_ge(S["vps"], (MT - 1) * which + m + 1)
                if is_act:
                    nc.scalar.activation(dst(m), PS[:, m % 6, 0:256], ACT.Copy, scale=RST[:, m:m + 1]).then_inc(S["vev_act"], 1)
                else:
                    nc.vector.tensor_scalar(dst(m), PS[:, m % 6, 0:256], RST[:, m:m + 1], None, ALU.mult).then_inc(S["vev_dve"], 1)

        def raw_count(s, j):
            return (s - j) // 2 + 1 if isinstance(s, int) else (s - j + 2) // 2

        PLAN_S = [0, 4, 7, 11, 14]
        PLAN_H = [[1, 7, 13, 18], [23, 29, 35, 40]]

        @block.sync
        def _(sp):
            def slab(s, j, nk, src):
                if not (isinstance(s, int) and s < 2):
                    sp.wait_ge(S["wh"], s - 1)
                    sp.wait_ge(S["wl"], s - 1)
                sp.dma_start(RAW[:, j, 0:nk * P], src).then_inc(S[f"raw{j}"], 16)

            def slabs(name, w, skip=0):
                s0, n, nk = PLAN.first[name], PLAN.count[name], PLAN.depth[name]

                def pair(i):
                    for j in range(2):
                        src = w[2 * i + j] if isinstance(i, int) else w[ds(2 * i + j, 1)].rearrange("a p n -> (a p) n")
                        slab(s0 + 2 * i + j, j, nk, src)
                loop(sp, skip, n // 2, pair)

            sp.dma_start(GAIN[:], t["gains"]).then_inc(S["gain"], 16)
            slabs("kA", t["w_kA"])
            for k in range(KT):
                sp.dma_start(XT[:, k * TOK:(k + 1) * TOK], t["xT"][k]).then_inc(xin[k], 16)
            sp.dma_start(IDN[:], t["ident"]).then_inc(S["const"], 16)
            slabs("vA", t["w_vA"])
            sp.wait_ge(S["sqs"], KT)
            sp.dma_start(TABA[:], t["tabA"]).then_inc(S["tabA"], 16)
            sp.dma_start(SINK[:], t["sinks"]).then_inc(S["tabA"], 16)
            slabs("qA", t["w_qA"])
            sp.wait_ge(S["stage"], 64)
            for a in range(2):
                sp.dma_start(KCA[:, :, a, :], t["ak_in"].rearrange("b (a p) k -> a p b k", a=2)[a]).then_inc(S["cA"], 16)
            sp.dma_start(VCA[:], t["av_in"].rearrange("b k d -> k b d")).then_inc(S["cA"], 16)
            sp.dma_start(TSA[:], t["tabSA"]).then_inc(S["tsa"], 16)
            sp.dma_start(SINKS[:, 0:1], t["sinkS"]).then_inc(S["tsa"], 16)
            slabs("oA", t["w_oA"])
            for c in range(len(FCH)):
                copies(sp, c)
                slabs(f"gu0{c}", t[f"w_gu0{c}"])
                slabs(f"dn0{c}", t[f"w_dn0{c}"])
            slabs("kB", t["w_kB"])
            slabs("vB", t["w_vB"])
            slabs("qB", t["w_qB"])
            sp.wait_ge(S["wl"], PLAN.end("qB"))
            sp.dma_start(TAB[0][:], t["tabB1"]).then_inc(S["tab1"], 16)
            sp.wait_ge(S["slab"], PLAN.end("qB"))
            sp.wait_ge(S["vst_out"], 32)
            vrow = t["bv"]
            sp.dma_start(VG[0][:], vrow[0:SEQ].rearrange("(n p) d -> p n d", p=P)).then_inc(S["vg0"], 16)
            v4 = vrow[0:SEQ].rearrange("(c p r) d -> r p c d", r=4, p=P)
            for r in range(4):
                sp.dma_start(VG[1][:, 2 * r:2 * r + 2, :], v4[r]).then_inc(S["vg1"], 16)
            u0 = t["u"][0].rearrange("(b h p) d -> b h p d", h=2, p=P)
            store_u(sp, 0, u0, 0, 0, 3)
            sp.wait_ge(S["stage"], 64 + 32)
            sp.dma_start(TAB[1][:], t["tabB4"]).then_inc(S["tab4"], 16)
            sp.dma_start(TAB[2][:], t["tabB16"]).then_inc(S["tab16"], 16)
            store_u(sp, 0, u0, 0, 3, 4)
            sp.wait_ge(S["pv"], 64 + 32)
            v16 = vrow[0:SEQ].rearrange("(i n r) d -> r i n d", r=2, n=8)
            for r in range(2):
                sp.dma_start(VG[0][64 * r:64 * r + 64, :, :], v16[r]).then_inc(S["vg0"], 16)
            store_u(sp, 4, t["u"][1].rearrange("(h p b) d -> b h p d", h=2, b=4), 1)
            sp.wait_ge(S["stage"], 64 + 64)
            sp.wait_ge(S["score"], 64 + 64)
            sp.wait_ge(S["rows_out"], 80)
            sp.dma_start(KC[:, 0], keys_of(0)).then_inc(S["kc0"], 16)
            sp.dma_start(VC[:, 1], values_of(1)).then_inc(S["vc1"], 16)
            sp.dma_start(TSB[:], t["tabSB"]).then_inc(S["tsb"], 16)
            sp.dma_start(TSW[:], t["tabSW"]).then_inc(S["tsb"], 16)
            u2 = t["u"][2].rearrange("(i b h r) d -> b h r i d", r=2, h=2, b=4)
            store_u(sp, 8, u2, 2, 0, 3)
            sp.wait_ge(S["stage"], 64 + 96)
            sp.dma_start(KC[:, 1], keys_of(1)).then_inc(S["kc1"], 16)
            sp.dma_start(VC[:, 0], values_of(0)).then_inc(S["vc0"], 16)
            store_u(sp, 8, u2, 2, 3, 4)
            sp.wait_ge(S["score"], 64 + 96)
            sp.wait_ge(S["ttr"], 64 + 96)
            sp.wait_ge(S["ust0"], 16 * 16)
            sp.wait_ge(S["ust1"], 16 * 16)

            def merge_load(b, j):
                src = t["u"][:, ds(b * P, P), :].rearrange("g p d -> p g d")
                sp.dma_start(MG[j][:], src).then_inc(S[f"mg{j}"], 16)
            merge_load(0, 0)
            merge_load(1, 1)

            def sample_loads(i):
                for j in range(2):
                    b = 2 * i + j
                    sp.wait_ge(S["sb_s"], b - 1)
                    sp.dma_start(KC[:, j], keys_of(b)).then_inc(S[f"kc{j}"], 16)
                    sp.wait_ge(S["sb_pv"], b - 1)
                    sp.dma_start(VC[:, j], values_of(b)).then_inc(S[f"vc{j}"], 16)
                    sp.wait_ge(S["m_om"], b - 1)
                    merge_load(b, j)
            loop(sp, 1, 4, sample_loads)
            slabs("oB", t["w_oB"])
            for c in range(len(FCH)):
                copies(sp, 4 + c)
                slabs(f"gu1{c}", t[f"w_gu1{c}"])
                slabs(f"dn1{c}", t[f"w_dn1{c}"])
            for k in range(KT):
                if k < 2 * YPOOL:
                    k = k // 2 if k % 2 == 0 else KT - YPOOL + k // 2
                else:
                    k -= YPOOL
                if k < KT - YPOOL:
                    sp.wait_ge(S["yt"], k + 1)
                else:
                    sp.wait_ge(S["yp"], k - (KT - YPOOL) + 1)
                sp.dma_start(t["yT"][k], YT[:, k, :]).then_inc(S["yout"], 16)
            sp.wait_ge(S["yout"], 16 * KT)
            sp.wait_ge(S["copies"], 16 * 18)
            sp.wait_ge(S["rows_out"], 16 * 5)

        @block.gpsimd
        def _(pool):
            nc.gpsimd.memset(EPSB[:], EPS).then_inc(S["eps"], 1)
            nc.gpsimd.memset(SQS[:, TOK:], 0.0).then_inc(S["pad"], 1)
            nc.gpsimd.memset(ONES[:], 1.0).then_inc(S["ones"], 1)
            pool.wait_ge(S["gain"], 16)

            def scale(name, gain, lo=0, hi=None):
                s0, n = PLAN.first[name], PLAN.count[name]

                def pair(i):
                    for j in range(2):
                        s = s0 + 2 * i + j
                        pool.wait_ge(S[f"raw{j}"], 16 * raw_count(s, j))
                        w = RAW[:, j, :].rearrange("p (k n) -> p k n", k=KT)
                        g = GAIN[:, gain * KT:(gain + 1) * KT].unsqueeze(2).to_broadcast([P, KT, P])
                        nc.gpsimd.tensor_tensor(w, w, g, ALU.mult).then_inc(S["scaled"], 1)
                loop(pool, lo, n // 2 if hi is None else hi, pair)
            scale("kA", 0)
            scale("vA", 0)
            scale("qA", 0, 0, 1)

            def stage(src, u):
                for kk in range(2):
                    r = slice(64 * kk, 64 * kk + 64)
                    ins = nc.gpsimd.tensor_copy(STG[r, 2 * u + kk, :], src[r])
                ins.then_inc(S["stage"], 1)

            def clear_stage(n):
                nc.gpsimd.memset(STG[:], 0.0).then_inc(S["clear"], 1)
                pool.wait_ge(S["clear"], n)

            def stage_a(i, first=False):
                for u in range(8):
                    if not first:
                        pool.wait_ge(S["score"], 8 * i + u - 7)
                    stage(QA[:, ds(u * SEQ + i * P, P)], u)

            groups_done(pool, "kA")
            ka = KA[:].rearrange("p (a n) -> p a n", a=2)
            pool.dma_start(t["akT"], ka[:, :, SEQ - P:TOK]).then_inc(S["rows_out"], 16)
            pool.wait_ge(S["vev_act"], 5)
            pool.wait_ge(S["vev_dve"], 4)
            pool.dma_start(t["avN"][0:P], VA[:, 7, :]).then_inc(S["rows_out"], 16)
            pool.dma_start(t["avN"][P:P + NEW], VA[0:NEW, 8, :]).then_inc(S["rows_out"], 16)
            scale("qA", 0, 1)
            groups_done(pool, "qA")
            clear_stage(1)
            stage_a(0, True)
            loop(pool, 1, 8, stage_a)
            pool.wait_ge(S["stage"], 64)
            for c in range(len(FCH)):
                scale(f"gu0{c}", 1)
            scale("kB", 2)
            scale("vB", 2)
            scale("qB", 3, 0, 1)
            groups_done(pool, "kB")
            pool.dma_start(t["bkT"], KB[:]).then_inc(S["rows_out"], 16)
            pool.dma_start(t["bkN"], KNB[:]).then_inc(S["rows_out"], 16)
            pool.wait_ge(S["vev_act"], 15)
            pool.wait_ge(S["vev_dve"], 12)
            pool.dma_start(t["bv"][0:SEQ].rearrange("(n p) d -> p n d", p=P), VST[:, 0:8, :]).then_inc(S["vst_out"], 16)
            pool.dma_start(t["bv"][SEQ:TOK], VST[0:NEW, 8, :]).then_inc(S["vst_out"], 16)
            scale("qB", 3, 1)
            groups_done(pool, "qB")
            clear_stage(2)

            def stage_b(g, i):
                for u in range(8):
                    pool.wait_ge(S["score"], 64 + 32 * g + 8 * i + u - 7)
                    stage(QB[:, ds((4 * g + u % 4) * SEQ + (2 * i + u // 4) * P, P)], u)

            def reorder(p, x):
                r = PATTERNS[1 + x][1]
                nc.gpsimd.tensor_copy(KP[x][:, ds(p * SEQ, SEQ)].rearrange("p (r i) -> p r i", r=r),
                                      KB[:, ds(p * SEQ, SEQ)].rearrange("p (i r) -> p r i", r=r)).then_inc(S["kperm"], 1)

            def stage_keys(i, first=False):
                for u in range(8):
                    if not first:
                        pool.wait_ge(S["score"], 64 + 8 * i + u - 7)
                    stage(QB[:, ds((u % 4) * SEQ + (2 * i + u // 4) * P, P)], u)
                    if u % 4 == 3:
                        x = u // 4
                        pool.wait_ge(S["stage"], 64 + 8 * i + u + 1)
                        reorder(i, x)
                        pool.wait_ge(S["kperm"], 2 * i + x + 1)
            pool.wait_ge(S["slab"], PLAN.end("qB"))
            stage_keys(0, True)
            loop(pool, 1, 4, stage_keys)
            for g in range(1, NG):
                loop(pool, 0, 4, lambda i: stage_b(g, i))
            pool.wait_ge(S["stage"], 64 + 96)
            nc.gpsimd.memset(SQN[:], 0.0).then_inc(S["sb_zero"], 1)
            pool.wait_ge(S["sb_zero"], 1)

            def sample(b, first, merged=None):
                if not first:
                    pool.wait_ge(S["sb_s"], b)
                if merged is not None:
                    pool.wait_ge(S["m_om"], merged)
                for kk in range(2):
                    src = QNB[64 * kk:64 * kk + 64, :, ds(b * NEWT, NEWT)]
                    dst = SQN[64 * kk:64 * kk + 64, :, :, 8 * kk:8 * kk + 8].rearrange("p g a n -> p (g a) n")
                    nc.gpsimd.tensor_copy(dst, src).then_inc(S["sb_stage"], 1)

            def merge(b, j, staged):
                pool.wait_ge(S["sb_stage"], 2 * staged)
                pool.wait_ge(S["m_c"], b + 1)
                c = SM[:, 64:88].unsqueeze(2).to_broadcast([P, 24, HD])
                for g in range(NG):
                    u = MG[j][:, g, 0:512].rearrange("p (h d) -> p h d", h=8)
                    nc.gpsimd.tensor_tensor(u, u, c[:, 8 * g:8 * g + 8, :], ALU.mult).then_inc(S["m_add"], 1)
                pool.wait_ge(S["m_add"], 4 * b + 3)
                nc.gpsimd.tensor_tensor(MG[j][:, 0, 0:512], MG[j][:, 0, 0:512], MG[j][:, 1, 0:512], ALU.add).then_inc(S["m_add"], 1)
                pool.wait_ge(S["m_add"], 4 * b + 4)
                if not (isinstance(b, int) and b == 0):
                    pool.wait_ge(S["m_tr"], b)
                nc.gpsimd.tensor_tensor(OM[:], MG[j][:, 0, 0:512], MG[j][:, 2, 0:512], ALU.add).then_inc(S["m_om"], 1)

            sample(0, True)
            sample(1, False)
            merge(0, 0, 2)
            sample(2, False, 1)
            merge(1, 1, 3)

            def pair(i):
                sample(2 * i + 1, False, 2 * i)
                merge(2 * i, 0, 2 * i + 2)
                sample(2 * i + 2, False, 2 * i + 1)
                merge(2 * i + 1, 1, 2 * i + 3)
            loop(pool, 1, 3, pair)
            sample(7, False, 6)
            merge(6, 0, 8)
            merge(7, 1, 8)
            for c in range(len(FCH)):
                scale(f"gu1{c}", 4)
            pool.wait_ge(S["rb"], PLAN_S[4] + 3)
            for n, k in enumerate(range(KT - YPOOL, KT)):
                pool.wait_ge(S["yg"], n + 1)
                nc.gpsimd.tensor_tensor(YT[:, k, :], YT[:, k, :], RB[:], ALU.mult).then_inc(S["yp"], 1)

        @block.scalar
        def _(act):
            def split_hi(name, x, j):
                s, nk = PLAN.first[name] + x, PLAN.depth[name]
                if not (isinstance(s, int) and s < 2):
                    act.wait_ge(S["slab"], s - 1)
                if name[:2] in ("oA", "oB", "dn"):
                    act.wait_ge(S[f"raw{j}"], 16 * raw_count(s, j))
                else:
                    act.wait_ge(S["scaled"], PLAN.scaled[name] + x + 1)
                nc.scalar.copy(WH[:, j, 0:nk * P], RAW[:, j, 0:nk * P]).then_inc(S["wh"], 1)

            def t_phase(name, evac, prefetch=True):
                s0, n = PLAN.first[name], PLAN.count[name]

                def pair(i, last=False):
                    for j in range(2):
                        if not last:
                            split_hi(name, 2 * i + j + 2, j)
                        elif prefetch and PLAN.next(name):
                            split_hi(PLAN.next(name), j, j)
                        if evac:
                            evac(i, j, s0 + 2 * i + j)
                loop(act, 0, n // 2 - 1, pair)
                pair(n // 2 - 1, True)

            def start(name):
                for j in range(2):
                    split_hi(name, j, j)

            def squares(norm, k, j):
                q = KT * norm + k
                if not (isinstance(k, int) and q < 2):
                    act.wait_ge(S["sqs"], q - 1)
                nc.scalar.activation(SQ[:, j, :], XT[:, ds(k * TOK, TOK)], ACT.Square).then_inc(S["sq"], 1)

            def high(k):
                nc.scalar.copy(XH[:, ds(k * TOK, TOK)], XT[:, ds(k * TOK, TOK)]).then_inc(S["xh"], 1)

            def after_o(norm, name):
                act.wait_ge(S["slab"], PLAN.end(name))
                for k in range(KT - 1):
                    high(k)
                act.wait_ge(S["free1"], PLAN.groups[name] + KT // 2)
                high(KT - 1)
                squares(norm, KT - 1, 1)

            def roots(norm, columns=False):
                for c, (a, w) in enumerate(CH):
                    act.wait_ge(S["sums"], PLAN_S[norm] + c + 1)
                    nc.scalar.activation(RB[:, a:a + w], PS[:, 6 + c % 2, 0:w], ACT.Sqrt, bias=EPSB[:],
                                         scale=1.0 / DM).then_inc(S["std"], 1)
                if columns:
                    act.wait_ge(S["sums"], PLAN_S[norm] + 4)
                    nc.scalar.activation(STD[:], PS[:, 7, 0:MT], ACT.Sqrt, bias=EPSB[:], scale=1.0 / DM).then_inc(S["std"], 1)

            start("kA")
            for k in range(KT):
                act.wait_ge(xin[k], 16)
                high(k)
                squares(0, k, k % 2)
            act.wait_ge(S["eps"], 1)
            roots(0, True)
            t_phase("kA", None)
            act.wait_ge(S["rb"], 4)
            v_phase(act, PLAN.first["vA"], 0, lambda m: VA[:, m, :], True)
            start("qA")
            t_phase("qA", None, prefetch=False)

            def attention(units0, n_bodies, peel, widths, finish):
                def exp_unit(i, u, w):
                    U = units0 + 8 * i + u
                    act.wait_ge(S["ttr"], U + 1)
                    for kk in range(2):
                        h = 2 * u + kk
                        ins = nc.scalar.activation(SB[:, u % 4, kk, 0:w], SB[:, u % 4, kk, 0:w], ACT.Exp,
                                                   bias=SM[:, h:h + 1], scale=-1.0, accum_out=SM[:, 16 + h:17 + h])
                    ins.then_inc(S["exp"], 1)

                def evac(i, u, w):
                    U = units0 + 8 * i + u
                    act.wait_ge(S["tr"], U + 1)
                    if not (isinstance(U, int) and U < 2):
                        act.wait_ge(S["pv"], U - 1)
                    nc.scalar.copy(PT[:, 1, 0:2 * w], PS[:, 3, 0:2 * w]).then_inc(S["pev1"], 1)

                def body(i, prev, cur=True, first=False, prev_first=False):
                    for st in range(8):
                        if cur:
                            exp_unit(i, st, widths(st, first))
                        v = (st - LAG) % 8
                        if v % 2 == 1 and (st >= LAG and cur):
                            evac(i, v, widths(v, first))
                        if v % 2 == 1 and st < LAG and prev is not None:
                            evac(prev, v, widths(v, prev_first))
                        if finish:
                            finish(i, prev, st, cur)
                body(0, None, first=True)
                if peel:
                    body(1, 0, prev_first=True)
                loop(act, 1 + peel, n_bodies, lambda i: body(i, i - 1))
                body(n_bodies, n_bodies - 1, cur=False)

            def finish_a(i, prev, st, cur):
                def es(b, h):
                    act.wait_ge(S["dsink"], 2 * b + h + 1)
                    nc.scalar.activation(SM[:, 48 + 8 * h:56 + 8 * h], SM[:, 32 + 8 * h:40 + 8 * h], ACT.Exp).then_inc(S["esink"], 1)

                def hi(b, h):
                    act.wait_ge(S["otr"], 2 * b + h + 1)
                    dst = XH[:, 0:KT * TOK].rearrange("p (k n) -> p k n", k=KT)[:, 4 * h:4 * h + 4, ds(b * P, P)]
                    nc.scalar.copy(dst, PS[:, 6 + h, :].rearrange("p (k n) -> p k n", k=4)).then_inc(S["ohi"], 1)
                if st == 4 and cur:
                    es(i, 0)
                if st == 0 and prev is not None:
                    es(prev, 1)
                if st == 2 and prev is not None:
                    hi(prev, 0)
                if st == 6 and prev is not None:
                    hi(prev, 1)

            act.wait_ge(S["slab"], PLAN.end("qA"))
            attention(0, 8, 1, lambda u, first: P if first else 256, finish_a)

            act.wait_ge(S["tsa"], 32)
            for b in range(NEWB):
                act.wait_ge(S["sa_ttr"], 2 * b + 2)
                nc.scalar.activation(PSA[:, b, :], PSA[:, b, :], ACT.Exp, bias=SM[:, b:b + 1], scale=-1.0,
                                     accum_out=SM[:, 16 + b:17 + b]).then_inc(S["sa_exp"], 1)
            nc.scalar.activation(SM[:, 32:40], SM[:, 0:8], ACT.Exp, bias=SINKS[:, 0:1]).then_inc(S["sa_es"], 1)
            for q in range(2):
                act.wait_ge(S["sa_tr"], q + 1)
                nc.scalar.copy(PTA[:, 4 * q:4 * q + 4, :], PS[:, 2 + q, :].rearrange("p (b n) -> p b n", b=4)).then_inc(S["sa_evA"], 1)
            for a in range(2):
                act.wait_ge(S["sa_pv"], a + 1)
                for kk in range(2):
                    src = PS[64 * kk:64 * kk + 64, 6 + a, :].rearrange("p (b k g i) -> p k g b i", b=8, k=2, g=4)[:, kk]
                    dst = XH[64 * kk:64 * kk + 64, 0:KT * TOK].rearrange("p (k n) -> p k n", k=KT)[:, 4 * a:4 * a + 4, SEQ:TOK]
                    nc.scalar.copy(dst.rearrange("p g (b i) -> p g b i", b=8), src).then_inc(S["sa_out"], 1)

            def evac_sq(norm, name, split=False):
                def evac(i, j, s):
                    k = 2 * i + j
                    if not split and isinstance(k, int) and k == KT - 1:
                        return
                    act.wait_ge(S[f"free{j}"], PLAN.groups[name] + i + 1)
                    squares(norm, k, j)
                    if split:
                        high(k)
                return evac
            act.wait_ge(S["pv"], 64)
            start("oA")
            t_phase("oA", evac_sq(1, "oA"))
            after_o(1, "oA")
            roots(1)
            act.wait_ge(S["rows_out"], 48)

            def ffn(l):
                for c, nf in enumerate(FCH):
                    h0, fill0 = PLAN_H[l][c], PLAN.groups[f"gu{l}{c}"]

                    def evac_gu(i, j, s, h0=h0, fill0=fill0):
                        if j == 0:
                            act.wait_ge(S["free0"], fill0 + i + 1)
                            nc.scalar.activation(GT[:], GT[:], ACT.Silu).then_inc(S["silu"], 1)
                        else:
                            act.wait_ge(S["free1"], fill0 + i + 1)
                            nc.scalar.copy(HH[:, ds(i * TOK, TOK)], HT[:]).then_inc(S["hh"], 1)
                    t_phase(f"gu{l}{c}", evac_gu)
                    if c == len(FCH) - 1:
                        t_phase(f"dn{l}{c}", evac_sq(2 + 2 * l, f"dn{l}{c}", split=l == 0))
                        if l == 1:
                            act.wait_ge(S["free1"], PLAN.groups[f"dn{l}{c}"] + KT // 2)
                            squares(4, KT - 1, 1)
                    else:
                        t_phase(f"dn{l}{c}", None)
            ffn(0)
            roots(2, True)

            t_phase("kB", None)
            act.wait_ge(S["rb"], PLAN_S[2] + 4)
            for q in range(2):
                v_phase(act, PLAN.first["vB"] + 2 * q, 1 + q, lambda m: VST[:, m, 256 * q:256 * q + 256], True)
                for j in range(2):
                    if q == 0:
                        split_hi("vB", 2 + j, j)
                    else:
                        split_hi("qB", j, j)
            t_phase("qB", None, prefetch=False)

            act.wait_ge(S["slab"], PLAN.end("qB"))
            for g in range(NG):
                attention(64 + 32 * g, 4, int(g == 0), widths_b(g), None)

            def sample(b, j):
                act.wait_ge(S["sb_ttr"], 4 * b + 4)
                nc.scalar.activation(PSB[:, j, :], PSB[:, j, :], ACT.Exp, bias=SM[:, 3:4], scale=-1.0,
                                     accum_out=SM[:, 8:9]).then_inc(S["sb_exp"], 1)

            def merge_w(b, j):
                act.wait_ge(S["m_d"], b + 1)
                nc.scalar.activation(SM[:, 40:64], SM[:, 40:64], ACT.Exp).then_inc(S["m_w"], 1)

            def sample_keys(b):
                act.wait_ge(S["sb_tr"], 2 * b + 1)
                if not (isinstance(b, int) and b == 0):
                    act.wait_ge(S["sb_pv"], b)
                nc.scalar.copy(PTS[:, 0:4, :], PS[:, 5, :].rearrange("p (c n) -> p c n", c=4)).then_inc(S["sb_evA"], 1)

            def sample_out(b):
                act.wait_ge(S["sb_pv"], b + 1)
                if not (isinstance(b, int) and b == 0):
                    act.wait_ge(S["sb_otr"], b)
                nc.scalar.copy(OS[:], PS[:, 7, 0:P]).then_inc(S["sb_os"], 1)
                act.wait_ge(S["sb_otr"], b + 1)
                for kk in range(2):
                    src = PS[64 * kk:64 * kk + 64, 2, 0:P].rearrange("p (a n) -> p a n", a=4)[:, :, 8 * kk:8 * kk + 8]
                    dst = XH[64 * kk:64 * kk + 64, 0:4 * TOK].rearrange("p (k n) -> p k n", k=4)[:, :, ds(SEQ + b * NEWT, NEWT)]
                    nc.scalar.copy(dst, src).then_inc(S["sb_oh"], 1)

            def merge_out(b):
                act.wait_ge(S["m_tr"], b + 1)
                dst = XH[:, 0:4 * TOK].rearrange("p (k n) -> p k n", k=4)[:, :, ds(b * P, P)]
                nc.scalar.copy(dst, PS[:, 0, :].rearrange("p (k n) -> p k n", k=4)).then_inc(S["m_hi"], 1)

            def batch(b, j):
                if not (isinstance(b, int) and b == 0):
                    sample_keys(b - 1)
                if not (isinstance(b, int) and b == NEWB):
                    sample(b, j)
                    merge_w(b, j)
                if not (isinstance(b, int) and b == 0):
                    sample_out(b - 1)
                if not (isinstance(b, int) and b < 2):
                    merge_out(b - 2)
            batch(0, 0)
            batch(1, 1)

            def pair(i):
                batch(2 * i, 0)
                batch(2 * i + 1, 1)
            loop(act, 1, 4, pair)
            batch(8, 0)
            merge_out(7)

            act.wait_ge(S["rows_out"], 80)
            start("oB")
            t_phase("oB", evac_sq(3, "oB"))
            after_o(3, "oB")
            roots(3)
            ffn(1)
            act.wait_ge(S["slab"], PLAN.end("dn13"))
            for k in range(KT - YPOOL, KT):
                g = GAIN[:, 5 * KT + k:5 * KT + k + 1]
                nc.scalar.activation(YT[:, k, :], XT[:, k * TOK:(k + 1) * TOK], ACT.Copy, scale=g).then_inc(S["yg"], 1)
                if k == KT - YPOOL:
                    roots(4)

        @block.vector
        def _(dve):
            def split_lo(s, j, nk):
                dve.wait_ge(S["wh"], s + 1)
                nc.vector.tensor_tensor(WL[:, j, 0:nk * P], RAW[:, j, 0:nk * P], WH[:, j, 0:nk * P].bitcast(F32),
                                        ALU.subtract).then_inc(S["wl"], 1)

            def t_phase(name, evac, prefetch=True, peel=False):
                s0, n, nk = PLAN.first[name], PLAN.count[name], PLAN.depth[name]

                def pair(i, last=False):
                    for j in range(2):
                        s = s0 + 2 * i + j
                        if not last:
                            split_lo(s + 2, j, nk)
                        elif prefetch and PLAN.next_depth(name):
                            split_lo(s + 2, j, PLAN.next_depth(name))
                        if evac:
                            evac(i, j, s)
                if peel:
                    pair(0)
                loop(dve, int(peel), n // 2 - 1, pair)
                pair(n // 2 - 1, True)

            def start(name):
                for j in range(2):
                    split_lo(PLAN.first[name] + j, j, PLAN.depth[name])

            def low(x, k, j=None):
                dve.wait_ge(S["xh"], KT * x + k + 1)
                nc.vector.tensor_tensor(XL[:, ds(k * TOK, TOK)], XT[:, ds(k * TOK, TOK)],
                                        XH[:, ds(k * TOK, TOK)].bitcast(F32), ALU.subtract).then_inc(S["xn"], 1)

            def add_squares(norm, k, j):
                dve.wait_ge(S["sq"], KT * norm + k + 1)
                if isinstance(k, int) and k == 0:
                    if norm:
                        dve.wait_ge(S["sums"], PLAN_S[norm])
                    nc.vector.tensor_copy(SQS[:, 0:TOK], SQ[:, 0, :]).then_inc(S["sqs"], 1)
                else:
                    dve.wait_ge(S["sqs"], KT * norm + k)
                    nc.vector.tensor_tensor(SQS[:, 0:TOK], SQS[:, 0:TOK], SQ[:, j, :], ALU.add).then_inc(S["sqs"], 1)

            def rstd(norm, columns=False):
                for c, (a, w) in enumerate(CH):
                    dve.wait_ge(S["std"], PLAN_S[norm] + c + 1)
                    nc.vector.reciprocal(RB[:, a:a + w], RB[:, a:a + w]).then_inc(S["rb"], 1)
                if columns:
                    dve.wait_ge(S["std"], PLAN_S[norm] + 4)
                    nc.vector.reciprocal(RST[:], STD[:]).then_inc(S["rb"], 1)
                dve.wait_ge(S["rb"], PLAN_S[norm] + 3 + columns)

            nc.vector.memset(XH[:, KT * TOK:].bitcast(F32), 0.0)
            nc.vector.memset(XL[:, KT * TOK:].bitcast(F32), 0.0)
            start("kA")
            for k in range(KT):
                low(0, k)
                add_squares(0, k, k % 2)
            rstd(0, True)

            def times_rms(dst, j, off, w):
                c = off // 384
                ps = PS[:, 3 * j:3 * j + 2, 0:384] if w == 768 else PS[:, 3 * j + c:3 * j + c + 1, off - 384 * c:off - 384 * c + w]
                return nc.vector.tensor_tensor(like(dst, w), ps, like(RB[:, off:off + w], w), ALU.mult)

            def evac_kA(i, j, s):
                dve.wait_ge(S["slab"], s + 1)
                times_rms(KA[:, j * TOK:j * TOK + 768], j, 0, 768)
                times_rms(KA[:, j * TOK + 768:(j + 1) * TOK], j, 768, 320).then_inc(S[f"free{j}"], 1)
            t_phase("kA", evac_kA)
            v_phase(dve, PLAN.first["vA"], 0, lambda m: VA[:, m, :], False)
            for j in range(2):
                split_lo(PLAN.first["qA"] + j, j, KT)

            def evac_rows(dst, new):
                def evac(i, j, s):
                    dve.wait_ge(S["slab"], s + 1)
                    n = 2 * i + j
                    times_rms(dst[:, ds(n * SEQ, 768)], j, 0, 768)
                    times_rms(dst[:, ds(n * SEQ + 768, 256)], j, 768, 256)
                    times_rms(new[:, ds(n, 1), :].rearrange("p a n -> p (a n)"), j, SEQ, NEW).then_inc(S[f"free{j}"], 1)
                return evac
            t_phase("qA", evac_rows(QA, QNA), prefetch=False)

            def attention(units0, n_bodies, peel, widths, table, loaded, init, stats, stats_read, norm, extra):
                first_of_all = lambda i: i == 0 and units0 in (0, 64)

                def scores(i, u, w):
                    U = units0 + 8 * i + u
                    dve.wait_ge(S["score"], U + 1)
                    if not (isinstance(U, int) and U < 4):
                        dve.wait_ge(S["tr"], U - 3)
                    if u % 4 == 0 and not (isinstance(i, int) and first_of_all(i)):
                        dve.wait_ge(*stats_read(i, u // 4))
                    dve.wait_ge(S[loaded], 16)
                    dve.sem_inc(S["turn"], 1)
                    for kk in range(2):
                        h = 2 * u + kk
                        ins = nc.vector.tensor_tensor_reduce(
                            out=SB[:, u % 4, kk, 0:w], in0=PS[:, u % 2, kk * w:(kk + 1) * w], in1=table(u, kk, w),
                            scale=-SCALE, scalar=init(h), op0=ALU.add, op1=ALU.min, accum_out=SM[:, h:h + 1])
                    ins.then_inc(S["ttr"], 1)

                def evac(i, u, w):
                    U = units0 + 8 * i + u
                    dve.wait_ge(S["tr"], U + 1)
                    if not (isinstance(U, int) and U < 2):
                        dve.wait_ge(S["pv"], U - 1)
                    nc.vector.tensor_copy(PT[:, 0, 0:2 * w], PS[:, 2, 0:2 * w]).then_inc(S["pev0"], 1)

                def body(i, prev, cur=True, first=False, prev_first=False):
                    for st in range(8):
                        if cur:
                            scores(i, st, widths(st, first))
                        v = (st - LAG) % 8
                        if v % 2 == 0 and st >= LAG and cur:
                            evac(i, v, widths(v, first))
                        if v % 2 == 0 and st < LAG and prev is not None:
                            evac(prev, v, widths(v, prev_first))
                        if st == LAG + 4 and cur:
                            stats(i, 0)
                        if st == LAG and prev is not None:
                            stats(prev, 1)
                        if st == PV_LAG + 3 - 8 and prev is not None:
                            norm(prev, 0)
                        if st == PV_LAG + 7 - 8 and prev is not None:
                            norm(prev, 1)
                        if extra:
                            extra(i, prev, st, cur)
                body(0, None, first=True)
                if peel:
                    body(1, 0, prev_first=True)
                loop(dve, 1 + peel, n_bodies, lambda i: body(i, i - 1))
                body(n_bodies, n_bodies - 1, cur=False)

            def stats_a(b, h):
                dve.wait_ge(S["esink"], 2 * b + h + 1)
                lo = 8 * h
                nc.vector.tensor_tensor(SM[:, 64 + lo:72 + lo], SM[:, 16 + lo:24 + lo], SM[:, 48 + lo:56 + lo], ALU.add).then_inc(S["rl"], 1)
                dve.wait_ge(S["rl"], 4 * b + 2 * h + 1)
                nc.vector.reciprocal(SM[:, 80 + lo:88 + lo], SM[:, 64 + lo:72 + lo]).then_inc(S["rl"], 1)

            def norm_a(b, h):
                lo = 8 * h
                dve.wait_ge(S["rl"], 4 * b + 2 * h + 2)
                dve.wait_ge(S["pv"], 8 * b + 4 * h + 4)
                if not (isinstance(b, int) and b == 0):
                    dve.wait_ge(S["otr"], 2 * b + h - 1)
                nc.vector.tensor_tensor(OSB[:, h, :].rearrange("p (a d) -> p a d", a=8),
                                        PS[:, 4 + h, :].rearrange("p (a d) -> p a d", a=8),
                                        SM[:, 80 + lo:88 + lo].unsqueeze(2).to_broadcast([P, 8, HD]),
                                        ALU.mult).then_inc(S[f"onorm{h}"], 1)

            def extra_a(i, prev, st, cur):
                def dsink(b, h):
                    lo = 8 * h
                    dve.wait_ge(S["ttr"], 8 * b + 4 * h + 4)
                    nc.vector.tensor_tensor(SM[:, 32 + lo:40 + lo], SM[:, lo:lo + 8], NSINK[:, lo:lo + 8],
                                            ALU.subtract).then_inc(S["dsink"], 1)

                def lo_part(b, h):
                    dve.wait_ge(S["ohi"], 2 * b + h + 1)
                    xl = XL[:, 0:KT * TOK].rearrange("p (k n) -> p k n", k=KT)[:, 4 * h:4 * h + 4, ds(b * P, P)]
                    xh = XH[:, 0:KT * TOK].rearrange("p (k n) -> p k n", k=KT)[:, 4 * h:4 * h + 4, ds(b * P, P)]
                    nc.vector.tensor_tensor(xl, PS[:, 6 + h, :].rearrange("p (k n) -> p k n", k=4),
                                            xh.bitcast(F32), ALU.subtract).then_inc(S["olo"], 1)
                if st == 3 and cur:
                    dsink(i, 0)
                if st == 7 and cur:
                    dsink(i, 1)
                if st == 3 and prev is not None:
                    lo_part(prev, 0)
                if st == 7 and prev is not None:
                    lo_part(prev, 1)

            dve.wait_ge(S["tabA"], 32)
            nc.vector.tensor_scalar(NSINK[:], SINK[:], -1.0, None, ALU.mult).then_inc(S["nsink"], 1)
            dve.wait_ge(S["nsink"], 1)
            dve.wait_ge(S["slab"], PLAN.end("qA"))
            attention(0, 8, 1, lambda u, first: P if first else 256,
                      lambda u, kk, w: TABA[:, 2 * u + kk, 256 - w:256], "tabA", lambda h: NSINK[:, h:h + 1], stats_a,
                      lambda i, h: (S["rl"], 4 * i - 2 + 2 * h), norm_a, extra_a)

            dve.wait_ge(S["tsa"], 32)
            nc.vector.tensor_scalar(SINKS[:, 1:2], SINKS[:, 0:1], -1.0, None, ALU.mult).then_inc(S["nsink"], 1)
            dve.wait_ge(S["nsink"], 2)
            dve.wait_ge(S["stage"], 64)
            for a in range(2):
                nc.vector.tensor_copy(QNS[:, a].rearrange("p b (g i) -> p b g i", g=4),
                                      QNA[:, 4 * a:4 * a + 4, :].rearrange("p g (b i) -> p b g i", b=NEWB)).then_inc(S["sa_q"], 1)
            for b in range(NEWB):
                dve.wait_ge(S["sa_s"], b + 1)
                nc.vector.tensor_tensor_reduce(out=PSA[:, b, 0:P], in0=PS[:, b % 2, 0:P], in1=TSA[:, 0:P], scale=-SCALE,
                                               scalar=SINKS[:, 1:2], op0=ALU.add, op1=ALU.min,
                                               accum_out=SM[:, 8 + b:9 + b]).then_inc(S["sa_ttr"], 1)
                dve.wait_ge(S["sa_ttr"], 2 * b + 1)
                w0 = P + 56 - 8 * b
                nc.vector.tensor_tensor_reduce(out=PSA[:, b, P:192], in0=PS[:, b % 2, P:192], in1=TSA[:, w0:w0 + 64],
                                               scale=-SCALE, scalar=SM[:, 8 + b:9 + b], op0=ALU.add, op1=ALU.min,
                                               accum_out=SM[:, b:b + 1]).then_inc(S["sa_ttr"], 1)
            dve.wait_ge(S["sa_es"], 1)
            nc.vector.tensor_tensor(SM[:, 40:48], SM[:, 16:24], SM[:, 32:40], ALU.add).then_inc(S["sa_p"], 1)
            dve.wait_ge(S["sa_p"], 1)
            nc.vector.reciprocal(SM[:, 48:56], SM[:, 40:48]).then_inc(S["sa_p"], 1)
            dve.wait_ge(S["sa_p"], 2)
            nc.vector.tensor_tensor(PSA[:], PSA[:], SM[:, 48:56].unsqueeze(2).to_broadcast([P, NEWB, 192]),
                                    ALU.mult).then_inc(S["sa_p"], 1)
            for q in range(2):
                dve.wait_ge(S["sa_tr"], 3 + q)
                nc.vector.tensor_copy(PTN[0:64, 4 * q:4 * q + 4, :], PS[0:64, 4 + q, :].rearrange("p (b n) -> p b n", b=4)).then_inc(S["sa_evD"], 1)
            for a in range(2):
                for kk in range(2):
                    dve.wait_ge(S["sa_out"], 2 * a + kk + 1)
                    src = PS[64 * kk:64 * kk + 64, 6 + a, :].rearrange("p (b k g i) -> p k g b i", b=8, k=2, g=4)[:, kk]
                    xh, xl = (X[64 * kk:64 * kk + 64, 0:KT * TOK].rearrange("p (k n) -> p k n", k=KT)[:, 4 * a:4 * a + 4, SEQ:TOK]
                              .rearrange("p g (b i) -> p g b i", b=8) for X in (XH, XL))
                    nc.vector.tensor_tensor(xl, src, xh.bitcast(F32), ALU.subtract).then_inc(S["sa_outlo"], 1)

            def add_residual(n, j, s):
                dve.wait_ge(S["slab"], s + 1)
                for ps, off, w in bank_parts(j):
                    x = like(XT[:, ds(n * TOK + off, w)], w)
                    ins = nc.vector.tensor_tensor(x, x, ps, ALU.add)
                ins.then_inc(S[f"free{j}"], 1)

            def evac_res(norm=None, split=False, late=False):
                def evac(i, j, s):
                    n = 2 * i + j
                    if late and isinstance(n, int) and n == KT - 1:
                        return
                    add_residual(n, j, s)
                    if norm is not None and not (isinstance(n, int) and n == 0):
                        add_squares(norm, n - 1, 1 - j)
                        if split:
                            low(norm, n - 1)
                return evac

            def after_o(norm, name):
                dve.wait_ge(S["slab"], PLAN.end(name))
                for k in range(KT - 3):
                    low(norm, k)
                add_residual(KT - 1, 1, PLAN.end(name) - 1)
                for k in range(KT - 3, KT):
                    low(norm, k)
                add_squares(norm, KT - 2, 0)
                add_squares(norm, KT - 1, 1)

            dve.wait_ge(S["pv"], 64)
            start("oA")
            t_phase("oA", evac_res(1, late=True), peel=True)
            after_o(1, "oA")
            rstd(1)
            dve.wait_ge(S["rows_out"], 48)

            def ffn(l):
                for c, nf in enumerate(FCH):
                    h0, fill0 = PLAN_H[l][c], PLAN.groups[f"gu{l}{c}"]

                    def evac_gu(i, j, s, h0=h0, fill0=fill0):
                        dve.wait_ge(S["slab"], s + 1)
                        if j == 0:
                            dve.wait_ge(S["free1"], fill0 + i)
                            times_rms(GT[:, 0:768], 0, 0, 768)
                            times_rms(GT[:, 768:TOK], 0, 768, 320).then_inc(S["free0"], 1)
                            dve.wait_ge(S["silu"], h0 + i)
                            nc.vector.tensor_tensor(GT[:], GT[:], RB[:], ALU.mult).then_inc(S["gt"], 1)
                            return
                        dve.wait_ge(S["gt"], h0 + i)
                        dve.wait_ge(S["hx"], h0 + i)
                        for n, (ps, off, w) in enumerate(bank_parts(1)):
                            ins = nc.vector.tensor_tensor(like(HT[:, off:off + w], w), like(GT[:, off:off + w], w), ps, ALU.mult)
                        ins.then_inc(S["free1"], 1)
                        dve.wait_ge(S["hh"], h0 + i)
                        nc.vector.tensor_tensor(HL[:, ds(i * TOK, TOK)], HT[:], HH[:, ds(i * TOK, TOK)].bitcast(F32),
                                                ALU.subtract).then_inc(S["hx"], 1)
                    t_phase(f"gu{l}{c}", evac_gu)
                    if c == len(FCH) - 1:
                        t_phase(f"dn{l}{c}", evac_res(2 + 2 * l, split=l == 0), peel=True)
                        add_squares(2 + 2 * l, KT - 1, 1)
                        if l == 0:
                            low(2, KT - 1)
                    else:
                        t_phase(f"dn{l}{c}", evac_res())
            dve.sem_inc(S["hx"], 1)
            ffn(0)
            rstd(2, True)

            t_phase("kB", evac_rows(KB, KNB))
            for q in range(2):
                v_phase(dve, PLAN.first["vB"] + 2 * q, 1 + q, lambda m: VST[:, m, 256 * q:256 * q + 256], False)
                for j in range(2):
                    split_lo(PLAN.first["vB"] + 2 * q + 2 + j, j, KT)
            dve.wait_ge(S["vev_act"], 15)
            nc.vector.tensor_copy(VNB[:], VST[:, 8, :]).then_inc(S["vnew"], 1)
            dve.wait_ge(S["vst_out"], 32)
            s0 = PLAN.first["qB"]
            for n in range(PLAN.count["qB"]):
                if n < PLAN.count["qB"] - 2:
                    split_lo(s0 + n + 2, n % 2, KT)
                dve.wait_ge(S["slab"], s0 + n + 1)
                store_q(n, n % 2, PATTERNS[n // 4][1])

            def stats_b(g):
                def stats(b, h):
                    n = 4 * g + b
                    dve.wait_ge(S["exp"], 64 + 8 * n + 4 * h + 4)
                    if not (isinstance(b, int) and n == 0):
                        dve.wait_ge(S[f"ust{h}"], 16 * (n if g < 2 else 8 + 2 * (n - 8)))
                    nc.vector.tensor_copy(UST[h][:, 512:520], SM[:, 8 * h:8 * h + 8])
                    nc.vector.tensor_copy(UST[h][:, 520:528], SM[:, 16 + 8 * h:24 + 8 * h]).then_inc(S["stat"], 1)
                return stats

            def norm_b(g):
                def norm(b, h):
                    dve.wait_ge(S["pv"], 64 + 32 * g + 8 * b + 4 * h + 4)
                    nc.vector.tensor_copy(UST[h][:, 0:512], PS[:, 4 + h, :]).then_inc(S[f"onorm{h}"], 1)
                return norm
            dve.wait_ge(S["slab"], PLAN.end("qB"))
            for g in range(NG):
                tab = TAB[g]
                full = 256 if g < 2 else P
                attention(64 + 32 * g, 4, int(g == 0), widths_b(g),
                          lambda u, kk, w: tab[:, 2 * (u % 4) + kk, full - w:full],
                          ("tab1", "tab4", "tab16")[g], lambda h: 1e38, stats_b(g),
                          lambda i, h: (S["stat"], 2 * (4 * g + i - 1) + h + 1), norm_b(g), None)

            dve.wait_ge(S["tsb"], 32)

            def sample(b, j):
                nc.vector.tensor_copy(TSN[:], TSW[:, :, ds(56 - 8 * b, NEW)]).then_inc(S["sb_tab"], 1)
                dve.wait_ge(S["sb_tab"], b + 1)
                dve.wait_ge(S["sb_s"], b + 1)
                segs = ((3, 0, R16, TSB[:, 0:512], 0), (4, 0, R4, TSB[:, 512:1024], 512), (1, 0, R1, TSB[:, 1024:1152], 1024))
                dve.sem_inc(S["turn"], 1)
                n = 0
                for bank, c0, w, tab, off in segs:
                    nc.vector.tensor_tensor_reduce(out=PSB[:, j, off:off + w], in0=PS[:, bank, c0:c0 + w], in1=tab,
                                                   scale=-SCALE, scalar=1e38 if n == 0 else SM[:, n - 1:n], op0=ALU.add,
                                                   op1=ALU.min, accum_out=SM[:, n:n + 1]).then_inc(S["sb_ttr"], 1)
                    n += 1
                    dve.wait_ge(S["sb_ttr"], 4 * b + n)
                    dve.sem_inc(S["turn"], 1)
                nc.vector.tensor_tensor_reduce(out=PSB[:, j, 1152:SCOLS].rearrange("p (g n) -> p g n", g=NG),
                                               in0=PS[:, 1, P:P + NG * NEW].rearrange("p (g n) -> p g n", g=NG),
                                               in1=TSN[:], scale=-SCALE, scalar=SM[:, 2:3],
                                               op0=ALU.add, op1=ALU.min, accum_out=SM[:, 3:4]).then_inc(S["sb_ttr"], 1)

            def weights(b, j):
                m = MG[j]
                dve.wait_ge(S[f"mg{j}"], 16 * ((b - j + 2) // 2) if not isinstance(b, int) else 16 * (b // 2 + 1))
                nc.vector.tensor_tensor(SM[:, 16:24], m[:, 0, 512:520], m[:, 1, 512:520], ALU.min).then_inc(S["m_min"], 1)
                dve.wait_ge(S["m_min"], 2 * b + 1)
                nc.vector.tensor_tensor(SM[:, 24:32], SM[:, 16:24], m[:, 2, 512:520], ALU.min).then_inc(S["m_min"], 1)
                dve.wait_ge(S["m_min"], 2 * b + 2)
                nc.vector.tensor_tensor(SM[:, 40:64].rearrange("p (g h) -> p g h", g=NG),
                                        SM[:, 24:32].unsqueeze(1).to_broadcast([P, NG, 8]), m[:, :, 512:520],
                                        ALU.subtract).then_inc(S["m_d"], 1)
                dve.wait_ge(S["m_w"], b + 1)
                nc.vector.tensor_tensor(SM[:, 16:40].rearrange("p (g h) -> p g h", g=NG),
                                        SM[:, 40:64].rearrange("p (g h) -> p g h", g=NG), m[:, :, 520:528],
                                        ALU.mult).then_inc(S["m_sum"], 1)
                dve.wait_ge(S["m_sum"], 3 * b + 1)
                nc.vector.tensor_reduce(SM[:, 88:96], SM[:, 16:40].rearrange("p (g h) -> p h g", g=NG),
                                        mybir.AxisListType.X, ALU.add).then_inc(S["m_sum"], 1)
                dve.wait_ge(S["m_sum"], 3 * b + 2)
                nc.vector.reciprocal(SM[:, 16:24], SM[:, 88:96]).then_inc(S["m_sum"], 1)
                dve.wait_ge(S["m_sum"], 3 * b + 3)
                if not (isinstance(b, int) and b == 0):
                    dve.wait_ge(S["m_om"], b)
                nc.vector.tensor_tensor(SM[:, 64:88].rearrange("p (g h) -> p g h", g=NG),
                                        SM[:, 40:64].rearrange("p (g h) -> p g h", g=NG),
                                        SM[:, 16:24].unsqueeze(1).to_broadcast([P, NG, 8]), ALU.mult).then_inc(S["m_c"], 1)

            def sums(b, j):
                q = PSB[:, j, :]
                dve.wait_ge(S["sb_exp"], b + 1)
                if not (isinstance(b, int) and b == 0):
                    dve.wait_ge(S["sb_tr"], 2 * b)
                nc.vector.reciprocal(SM[:, 9:10], SM[:, 8:9]).then_inc(S["sb_p"], 1)
                nc.vector.tensor_tensor(q[:, 512:768], q[:, 512:768], q[:, 256:512], ALU.add).then_inc(S["sb_p"], 1)
                nc.vector.tensor_tensor(q[:, 1152:1216], q[:, 1152:1216], q[:, 1216:1280], ALU.add).then_inc(S["sb_p"], 1)
                dve.wait_ge(S["sb_p"], 6 * b + 3)
                r1 = q[:, 512:1024].rearrange("p (c n) -> p c n", c=2)[:, :, 192:256]
                nc.vector.tensor_tensor(r1, r1, q[:, 1024:1152].rearrange("p (c n) -> p c n", c=2), ALU.add).then_inc(S["sb_p"], 1)
                nc.vector.tensor_tensor(q[:, 1152:1216], q[:, 1152:1216], q[:, 1280:1344], ALU.add).then_inc(S["sb_p"], 1)
                dve.wait_ge(S["sb_p"], 6 * b + 5)
                rl = SM[:, 9:10]
                nc.vector.tensor_scalar(PNB[:, 0:256], q[:, 0:256], rl, None, ALU.mult)
                nc.vector.tensor_scalar(PNB[:, 256:768], q[:, 512:1024], rl, None, ALU.mult)
                nc.vector.tensor_scalar(PNB[:, 768:832], q[:, 1152:1216], rl, None, ALU.mult).then_inc(S["sb_p"], 1)

            def sample_keys(b):
                dve.wait_ge(S["sb_tr"], 2 * b + 2)
                if not (isinstance(b, int) and b == 0):
                    dve.wait_ge(S["sb_pv"], b)
                nc.vector.tensor_copy(PTS[:, 4:6, :], PS[:, 6, 0:256].rearrange("p (c n) -> p c n", c=2)).then_inc(S["sb_evD"], 1)
                nc.vector.tensor_copy(PTS[0:64, 6, :], PS[0:64, 6, 256:384]).then_inc(S["sb_evD"], 1)

            def sample_out(b):
                for kk in range(2):
                    dve.wait_ge(S["sb_oh"], 2 * b + kk + 1)
                    src = PS[64 * kk:64 * kk + 64, 2, 0:P].rearrange("p (a n) -> p a n", a=4)[:, :, 8 * kk:8 * kk + 8]
                    hi, lo = (XH[64 * kk:64 * kk + 64, z * TOK:(z + 4) * TOK].rearrange("p (k n) -> p k n", k=4)[:, :, ds(SEQ + b * NEWT, NEWT)]
                              for z in (0, 4))
                    nc.vector.tensor_tensor(lo, src, hi.bitcast(F32), ALU.subtract).then_inc(S["sb_ol"], 1)

            def merge_out(b):
                dve.wait_ge(S["m_hi"], b + 1)
                hi, lo = (XH[:, z * TOK:(z + 4) * TOK].rearrange("p (k n) -> p k n", k=4)[:, :, ds(b * P, P)] for z in (0, 4))
                nc.vector.tensor_tensor(lo, PS[:, 0, :].rearrange("p (k n) -> p k n", k=4), hi.bitcast(F32),
                                        ALU.subtract).then_inc(S["m_lo"], 1)

            def batch(b, j):
                if not (isinstance(b, int) and b == 0):
                    sample_keys(b - 1)
                if not (isinstance(b, int) and b == NEWB):
                    sample(b, j)
                    weights(b, j)
                    sums(b, j)
                if not (isinstance(b, int) and b == 0):
                    sample_out(b - 1)
                if not (isinstance(b, int) and b < 2):
                    merge_out(b - 2)
            batch(0, 0)
            batch(1, 1)

            def pair(i):
                batch(2 * i, 0)
                batch(2 * i + 1, 1)
            loop(dve, 1, 4, pair)
            batch(8, 0)
            merge_out(7)

            start("oB")
            dve.wait_ge(S["rows_out"], 80)
            t_phase("oB", evac_res(3, late=True), peel=True)
            after_o(3, "oB")
            rstd(3)
            ffn(1)
            rstd(4)
            for k in range(KT - YPOOL):
                nc.vector.scalar_tensor_tensor(YT[:, k, :], XT[:, k * TOK:(k + 1) * TOK],
                                               GAIN[:, 5 * KT + k:5 * KT + k + 1], RB[:], ALU.mult, ALU.mult).then_inc(S["yt"], 1)

        @block.tensor
        def _(pe):
            mm = nc.tensor.matmul

            def tiles(x, first=0):
                return lambda k, a, n: x[:, (k + first) * TOK + a:(k + first) * TOK + a + n]

            def slab(s, j, nk, hi, lo, fill, operand):
                pe.wait_ge(S["wl"], s + 1)
                if not (isinstance(fill, int) and fill == 0):
                    pe.wait_ge(S[f"free{j}"], fill)
                for k in range(nk):
                    if operand:
                        operand(k)
                    for n, (w, x) in enumerate(((WH, hi), (WH, lo), (WL, hi))):
                        for c, (a, width) in enumerate(CH):
                            ins = mm(PS[:, 3 * j + c, 0:width], w[:, j, k * P:(k + 1) * P], x(k, a, width),
                                     start=(k == 0 and n == 0), stop=(k == nk - 1 and n == 2))
                ins.then_inc(S["slab"], 1)

            def t_phase(name, hi, lo, operand, norm=None, columns=False):
                s0, n, nk, g0 = PLAN.first[name], PLAN.count[name], PLAN.depth[name], PLAN.groups[name]

                def pair(i):
                    for j in range(2):
                        slab(s0 + 2 * i + j, j, nk, hi, lo, g0 + i, operand)
                        if norm is not None and isinstance(i, int) and i + j == 0:
                            sums(norm, columns)
                if norm is not None:
                    pair(0)
                loop(pe, 0 if norm is None else 1, n // 2, pair)

            def sums(norm, columns=False):
                pe.wait_ge(S["sqs"], KT * (norm + 1))
                for c, (a, w) in enumerate(CH):
                    if c == 2:
                        pe.wait_ge(S["std"], PLAN_S[norm] + 1)
                    mm(PS[:, 6 + c % 2, 0:w], ONES[:], SQS[:, a:a + w], start=True, stop=True).then_inc(S["sums"], 1)
                if columns:
                    pe.wait_ge(S["std"], PLAN_S[norm] + 2)
                    for m in range(MT):
                        ins = mm(PS[:, 7, m:m + 1], SQS[:, m * P:(m + 1) * P], ONES[:, 0:1], start=True, stop=True)
                    ins.then_inc(S["sums"], 1)

            def v_phase(s, which, after):
                groups_done(pe, after)
                pe.wait_ge(S["wl"], s + 2)
                for m in range(MT):
                    if m < 6 and which:
                        pe.wait_ge(S["vev_act"], 5 * which)
                        pe.wait_ge(S["vev_dve"], 4 * which)
                    if m >= 6:
                        pe.wait_ge(S["vev_dve" if m % 2 else "vev_act"], (4 if m % 2 else 5) * which + (m - 6) // 2 + 1)
                    for k in range(KT):
                        for n, (w, x) in enumerate(((WH, XH), (WH, XL), (WL, XH))):
                            ins = mm(PS[:, m % 6, 0:256].rearrange("p (a n) -> p a n", a=2),
                                     x[:, k * TOK + m * P:k * TOK + (m + 1) * P], w[:, :, k * P:(k + 1) * P],
                                     start=(k == 0 and n == 0), stop=(k == KT - 1 and n == 2))
                    if m == MT - 1:
                        ins.then_inc(S["slab"], 2)
                    else:
                        ins.then_inc(S["vps"], 1)

            def v_read(which):
                pe.wait_ge(S["vev_act"], 5 * which)
                pe.wait_ge(S["vev_dve"], 4 * which)

            def xn_ready(x):
                return lambda k: pe.wait_ge(S["xn"], KT * x + k + 1)
            XHT, XLT = tiles(XH), tiles(XL)

            pe.wait_ge(S["ones"], 1)
            pe.wait_ge(S["pad"], 1)
            t_phase("kA", XHT, XLT, xn_ready(0), 0, True)
            v_phase(PLAN.first["vA"], 0, "kA")
            v_read(1)
            t_phase("qA", XHT, XLT, None)

            def attention(units0, n_bodies, peel, widths, keys, values, finish, loaded=None):
                def scores(i, u, w, first):
                    U = units0 + 8 * i + u
                    pe.wait_ge(S["stage"], U + 1)
                    if not (isinstance(U, int) and U < 2):
                        pe.wait_ge(S["ttr"], U - 1)
                    for kk in range(2):
                        ins = mm(PS[:, u % 2, kk * w:(kk + 1) * w], STG[:, 2 * u + kk, :], keys(i, u, w, first),
                                 start=True, stop=True)
                    ins.then_inc(S["score"], 1)

                def transposes(i, u, w):
                    U = units0 + 8 * i + u
                    pe.wait_ge(S["exp"], U + 1)
                    if not (isinstance(U, int) and U < 2):
                        pe.wait_ge(S[f"pev{u % 2}"], units0 // 2 + 4 * i + u // 2)
                    for kk in range(2):
                        for c in range(w // P):
                            ins = nc.tensor.transpose(PS[:, 2 + u % 2, kk * w + c * P:kk * w + (c + 1) * P],
                                                      SB[:, u % 4, kk, c * P:(c + 1) * P], IDN[:])
                    ins.then_inc(S["tr"], 1)

                def pv(i, u, w, first):
                    pe.wait_ge(S[f"pev{u % 2}"], units0 // 2 + 4 * i + u // 2 + 1)
                    if u % 4 == 0 and not (isinstance(i, int) and units0 + i == 0):
                        pe.wait_ge(S[f"onorm{u // 4}"], units0 // 8 + i)
                    for kk in range(2):
                        o = (2 * (u % 4) + kk) * HD
                        for c in range(w // P):
                            ins = mm(PS[:, 4 + u // 4, o:o + HD], PT[:, u % 2, kk * w + c * P:kk * w + (c + 1) * P],
                                     values(i, u, kk, c, w, first), start=(c == 0), stop=(c == w // P - 1))
                    ins.then_inc(S["pv"], 1)

                def body(i, prev, cur=True, first=False, prev_first=False):
                    for st in range(8):
                        if cur:
                            scores(i, st, widths(st, first), first)
                        for lag, what in ((LAG, transposes), (PV_LAG, pv)):
                            v = (st - lag) % 8
                            own = st >= lag
                            if own and not cur or not own and prev is None:
                                continue
                            b, f = (i, first) if own else (prev, prev_first)
                            if what is pv:
                                if loaded and first and v == 0:
                                    loaded()
                                pv(b, v, widths(v, f), f)
                            else:
                                transposes(b, v, widths(v, f))
                        if finish:
                            finish(i, prev, st, cur)
                body(0, None, first=True)
                if peel:
                    body(1, 0, prev_first=True)
                loop(pe, 1 + peel, n_bodies, lambda i: body(i, i - 1))
                body(n_bodies, n_bodies - 1, cur=False)

            def finish_a(i, prev, st, cur):
                def otr(b, h):
                    pe.wait_ge(S[f"onorm{h}"], b + 1)
                    if not (isinstance(b, int) and b == 0):
                        pe.wait_ge(S["olo"], 2 * b + h - 1)
                    for c in range(4):
                        ins = nc.tensor.transpose(PS[:, 6 + h, c * P:(c + 1) * P], OSB[:, h, c * P:(c + 1) * P], IDN[:])
                    ins.then_inc(S["otr"], 1)
                if st == 1 and prev is not None:
                    otr(prev, 0)
                if st == 5 and prev is not None:
                    otr(prev, 1)

            def keys_a(i, u, w, first):
                a = u // 4
                return KA[:, ds(a * TOK + (0 if first else (i - 1) * P), w)]

            def values_a(i, u, kk, c, w, first):
                a = u // 4
                m = 0 if first else i - 1 + c
                d = (2 * a + kk) * HD
                return VA[:, ds(m, 1), d:d + HD].rearrange("p m d -> p (m d)")

            groups_done(pe, "qA")
            attention(0, 8, 1, lambda u, first: P if first else 256, keys_a, values_a, finish_a)

            pe.wait_ge(S["cA"], 48)
            pe.wait_ge(S["sa_q"], 2)
            for b in range(NEWB):
                if b >= 2:
                    pe.wait_ge(S["sa_ttr"], 2 * b - 2)
                for a in range(2):
                    for kk in range(2):
                        r, o = slice(64 * kk, 64 * kk + 64), 32 * (2 * a + kk)
                        q = QNS[r, a, b, :]
                        mm(PS[o:o + 32, b % 2, 0:P], q, KCA[r, b, a, :], start=True, stop=True)
                        ins = mm(PS[o:o + 32, b % 2, P:192], q, KA[r, a * TOK + SEQ:(a + 1) * TOK], start=True, stop=True)
                ins.then_inc(S["sa_s"], 1)
            pe.wait_ge(S["sa_p"], 3)
            for q in range(2):
                for b in range(4):
                    ins = nc.tensor.transpose(PS[:, 2 + q, b * P:(b + 1) * P], PSA[:, 4 * q + b, 0:P], IDN[:])
                ins.then_inc(S["sa_tr"], 1)
            for q in range(2):
                for b in range(4):
                    ins = nc.tensor.transpose(PS[0:64, 4 + q, b * P:(b + 1) * P], PSA[:, 4 * q + b, P:192], IDN[:])
                ins.then_inc(S["sa_tr"], 1)
            pe.wait_ge(S["sa_evA"], 2)
            pe.wait_ge(S["sa_evD"], 2)
            pe.wait_ge(S["olo"], 16)
            for a in range(2):
                for b in range(NEWB):
                    o = PS[:, 6 + a, b * 64:(b + 1) * 64]
                    mm(o, VCA[:, b, a * P:(a + 1) * P], PTA[:, b, a * 64:(a + 1) * 64], start=True, stop=False)
                    ins = mm(o, VA[0:NEW, 8, a * P:(a + 1) * P], PTN[0:NEW, b, a * 64:(a + 1) * 64], start=False, stop=True)
                ins.then_inc(S["sa_pv"], 1)

            pe.wait_ge(S["sa_outlo"], 4)
            t_phase("oA", XHT, XLT, None)

            def ffn(l):
                for c, nf in enumerate(FCH):
                    h0 = PLAN_H[l][c]
                    norm = 1 + 2 * l if c == 0 else None
                    t_phase(f"gu{l}{c}", XHT, XLT, xn_ready(norm) if c == 0 else None, norm)
                    t_phase(f"dn{l}{c}", tiles(HH), tiles(HL), lambda k: pe.wait_ge(S["hx"], h0 + k + 1))
            ffn(0)

            t_phase("kB", XHT, XLT, xn_ready(2), 2, True)
            for q in range(2):
                v_phase(PLAN.first["vB"] + 2 * q, 1 + q, "kB")
            v_read(3)
            t_phase("qB", XHT, XLT, None)
            groups_done(pe, "qB")

            def keys_b(g):
                src = KB if g == 0 else KP[g - 1]

                def keys(i, u, w, first):
                    p, h = u % 4, u // 4
                    if g == 0:
                        off = 0 if first and h == 0 else (2 * i - 1 + h) * P
                    elif g == 1:
                        off = 2 * i * P
                    else:
                        off = (2 * i + h) * P
                    return src[:, ds(p * SEQ + off, w)]
                return keys

            def values_b(g):
                def values(i, u, kk, c, w, first):
                    p, h = u % 4, u // 4
                    if g == 0:
                        m = 0 if first and h == 0 else 2 * i - 1 + h + c
                    elif g == 1:
                        m = 2 * i + c
                    else:
                        m = 2 * i + h
                    d = (2 * p + kk) * HD
                    return VG[g % 2][:, ds(m, 1), d:d + HD].rearrange("p m d -> p (m d)")
                return values
            for g in range(NG):
                if g:
                    pe.wait_ge(S["kperm"], 8)
                attention(64 + 32 * g, 4, int(g == 0), widths_b(g), keys_b(g), values_b(g), None,
                          lambda: pe.wait_ge(S[f"vg{g % 2}"], (16, 64, 48)[g]))

            def sample_scores(b, j):
                pe.wait_ge(S["sb_stage"], 2 * b + 2)
                pe.wait_ge(S[f"kc{j}"], 16 * raw_count(b, j))
                if not (isinstance(b, int) and b == 0):
                    pe.wait_ge(S["sb_ttr"], 4 * b)
                for p in range(4):
                    o = slice(32 * p, 32 * p + 32)
                    mm(PS[o, 3, 0:512], SQN[:, 2, p, :], KC[:, j, p, 0:512], start=True, stop=True)
                    mm(PS[o, 4, 0:512], SQN[:, 1, p, :], KC[:, j, p, 256:768], start=True, stop=True)
                    k1 = KC[:, j, p, 256:768].rearrange("p (c n) -> p c n", c=2)[:, :, 192:256]
                    mm(PS[o, 1, 0:P].rearrange("p (c n) -> p c n", c=2), SQN[:, 0, p, :], k1, start=True, stop=True)
                    for g in range(NG):
                        c0 = P + g * NEW
                        ins = mm(PS[o, 1, c0:c0 + NEW], SQN[:, g, p, :], KNB[:, p, :], start=True, stop=True)
                ins.then_inc(S["sb_s"], 1)

            def merged(b):
                pe.wait_ge(S["m_om"], b + 1)
                if not (isinstance(b, int) and b == 0):
                    pe.wait_ge(S["m_lo"], b)
                for c in range(4):
                    ins = nc.tensor.transpose(PS[:, 0, c * P:(c + 1) * P], OM[:, c * P:(c + 1) * P], IDN[:])
                ins.then_inc(S["m_tr"], 1)

            def sample_values(b, j, first=False):
                pe.wait_ge(S["sb_p"], 6 * b + 6)
                if not (isinstance(b, int) and b == 0):
                    pe.wait_ge(S["sb_evA"], b)
                    pe.wait_ge(S["sb_evD"], 2 * b)
                for c in range(4):
                    ins = nc.tensor.transpose(PS[:, 5, c * P:(c + 1) * P], PNB[:, c * P:(c + 1) * P], IDN[:])
                ins.then_inc(S["sb_tr"], 1)
                for c in range(2):
                    nc.tensor.transpose(PS[:, 6, c * P:(c + 1) * P], PNB[:, (4 + c) * P:(5 + c) * P], IDN[:])
                nc.tensor.transpose(PS[0:NEW, 6, 256:384], PNB[:, KEPT:KEPT + NEW], IDN[:]).then_inc(S["sb_tr"], 1)
                pe.wait_ge(S["sb_evA"], b + 1)
                pe.wait_ge(S["sb_evD"], 2 * b + 2)
                pe.wait_ge(S[f"vc{j}"], 16 * raw_count(b, j))
                if not (isinstance(b, int) and b == 0):
                    pe.wait_ge(S["sb_os"], b)
                for c in range(7):
                    for p in range(4):
                        o = PS[32 * p:32 * p + 32, 7, 0:P]
                        f = slice(p * P, (p + 1) * P)
                        if c < 6:
                            mm(o, PTS[:, c, 32 * p:32 * p + 32], VC[:, j, c, f], start=(c == 0), stop=False)
                        else:
                            ins = mm(o, PTS[0:NEW, 6, 32 * p:32 * p + 32], VNB[0:NEW, f], start=False, stop=True)
                ins.then_inc(S["sb_pv"], 1)
                if not first:
                    merged(b - 1)
                pe.wait_ge(S["sb_os"], b + 1)
                if not (isinstance(b, int) and b == 0):
                    pe.wait_ge(S["sb_ol"], 2 * b)
                nc.tensor.transpose(PS[:, 2, 0:P], OS[:], IDN[:]).then_inc(S["sb_otr"], 1)

            pe.wait_ge(S["onorm0"], 8 + 12)
            pe.wait_ge(S["onorm1"], 8 + 12)
            sample_scores(0, 0)
            sample_scores(1, 1)
            sample_values(0, 0, True)
            sample_scores(2, 0)
            sample_values(1, 1)

            def pair(i):
                sample_scores(2 * i + 1, 1)
                sample_values(2 * i, 0)
                sample_scores(2 * i + 2, 0)
                sample_values(2 * i + 1, 1)
            loop(pe, 1, 3, pair)
            sample_scores(7, 1)
            sample_values(6, 0)
            sample_values(7, 1)
            merged(7)

            pe.wait_ge(S["sb_ol"], 16)
            pe.wait_ge(S["m_lo"], 8)
            t_phase("oB", tiles(XH), tiles(XH, 4), None)
            ffn(1)
            sums(4)


def slopes(n):
    return np.asarray(2.0 ** (-8.0 * (np.arange(n) + 1) / n), dtype=np.float32)


def penalty(slope, dist, valid):
    d = -(np.float32(slope) * dist.astype(np.float32)) * np.float32(UNSCALE)
    return np.where(valid, d, np.float32(NEG)).astype(np.float32)


def key_order():
    k = np.arange(PAST)
    low, near = k % 16 < 8, k >= PAST // 2
    return np.concatenate([k[low & ~near], k[low & near], k[~low & near], k[~low & ~near]])


def a_head(u, kk):
    return A_GRP * (2 * (u // A_GRP) + kk) + u % A_GRP


def host_tables():
    sa, sb = slopes(A_HEADS), slopes(NG * B_SLOTS).reshape(NG, B_SLOTS)
    q, k = np.arange(P)[:, None], np.arange(256)[None, :]
    d = P + q - k
    t = {}
    order = [a_head(u, kk) for u in range(8) for kk in range(2)]
    t["tabA"] = np.stack([penalty(sa[h], d, (d >= 0) & (d < P)) for h in order], 1)
    for g, name in ((0, "tabB1"), (1, "tabB4")):
        r = PATTERNS[g][1]
        t[name] = np.stack([penalty(sb[g, h], r * d, (d >= 0) & (d <= P)) for h in range(B_SLOTS)], 1)
    d = q - np.arange(P)[None, :]
    same = (q // 64) == (np.arange(P)[None, :] // 64)
    t["tabB16"] = np.stack([penalty(sb[2, h], 16 * d, (d >= 0) & same) for h in range(B_SLOTS)], 1)
    row = np.arange(P)
    i = row % 8
    sl = sa[row // 8][:, None]
    dc = P + i[:, None] - np.arange(P)[None, :]
    w = np.arange(120)[None, :] - 56
    dn = i[:, None] - w
    new = (w >= 0) & (w < 8) & (dn >= 0)
    t["tabSA"] = np.concatenate([penalty(sl, dc, (dc >= 0) & (dc < P)), penalty(sl, dn, new)], 1)
    used = (row % 32 < 16)[:, None]
    head = 2 * (row // 32) + (row % 32 // 8) % 2
    pos = PAST + i[:, None]
    ko = key_order()
    seg = []
    for g, keys in ((2, ko[0:512]), (1, ko[256:768]), (0, np.concatenate([ko[448:512], ko[704:768]]))):
        wdw, r = PATTERNS[g]
        dist = pos - keys[None, :]
        ok = (dist >= 0) & (dist <= wdw) & (dist % r == 0)
        seg.append(np.where(used, penalty(sb[g, head][:, None], dist, ok), 0))
    t["tabSB"] = np.concatenate(seg, 1).astype(np.float32)
    t["tabSW"] = np.stack([np.where(used, penalty(sb[g, head][:, None], dn, new & (dn % PATTERNS[g][1] == 0)), 0)
                           for g in range(NG)], 1).astype(np.float32)
    t["ident"] = np.eye(P, dtype=np.float32)
    return t


def slab_layout(w, cols):
    k = w.shape[0] // P
    return np.ascontiguousarray(w.reshape(k, P, -1)[:, :, cols].transpose(2, 1, 0, 3).reshape(len(cols), P, k * P))


def kernel(**inputs):
    import concourse.bacc as bacc
    from concourse.bass_utils import run_bass_kernel_spmd

    x = {n: np.asarray(a) for n, a in inputs.items()}
    feed = host_tables()
    cont = np.ascontiguousarray
    tokens = np.concatenate([x["x_prompt"].reshape(SEQ, DM), x["x_sample"].reshape(NEW, DM)], 0)
    feed["xT"] = cont(tokens.T.reshape(KT, P, TOK))
    gains = np.stack([x["g_attn"][0], x["g_ffn"][0], x["g_kv"], x["g_attn"][1], x["g_ffn"][1], x["g_final"]])
    feed["gains"] = cont(gains.reshape(6, KT, P).transpose(2, 0, 1).reshape(P, 6 * KT))
    sinks = x["sinks_a"][0]
    order = [a_head(u, kk) for u in range(8) for kk in range(2)]
    feed["sinks"] = cont(np.broadcast_to(sinks[order], (P, 16)))
    feed["sinkS"] = cont(np.repeat(sinks, 8)[:, None])
    tile = lambda n0, n: n0 + np.arange(n * P).reshape(n, P)
    wa = x["w_qkv_a"][0]
    hcol = np.array([[a_head(u, kk) * HD + d for kk in range(2) for d in range(HD)] for u in range(8)])
    feed["w_kA"], feed["w_vA"] = slab_layout(wa, tile(1024, 2)), slab_layout(wa, tile(1280, 2))
    feed["w_qA"] = slab_layout(wa, hcol)
    feed["w_oA"] = slab_layout(x["w_o_a"][0][hcol.reshape(-1)], tile(0, 8))
    feed["w_kB"], feed["w_vB"] = slab_layout(x["w_kv_s"], tile(0, 4)), slab_layout(x["w_kv_s"], tile(512, 4))
    feed["w_qB"] = slab_layout(x["w_q_b"][0], tile(0, 12))
    feed["w_oB"] = slab_layout(x["w_o_b"][0], tile(0, 8))
    for l in range(2):
        gu, dn = x["w_gate_up"][l], x["w_down"][l]
        f0 = 0
        for c, n in enumerate(FCH):
            cols = np.stack([tile(f0 * P, n), tile(DFF + f0 * P, n)], 1).reshape(2 * n, P)
            feed[f"w_gu{l}{c}"] = slab_layout(gu, cols)
            feed[f"w_dn{l}{c}"] = slab_layout(dn[f0 * P:(f0 + n) * P], tile(0, 8))
            f0 += n
    ko = key_order()
    feed["ak_in"] = cont(x["cache_a_k"][0].reshape(NEWB, P, 256).transpose(0, 2, 1))
    feed["av_in"] = cont(x["cache_a_v"][0].reshape(NEWB, P, 256))
    feed["bk_in"] = cont(x["cache_b_k"].reshape(NEWB, PAST, 512)[:, ko].transpose(0, 2, 1))
    feed["bv_in"] = cont(x["cache_b_v"].reshape(NEWB, PAST, 512)[:, ko])
    outs = {"yT": (KT, P, TOK), "akT": (P, 2, P + NEW), "avN": (P + NEW, 256), "akS": (NEWB, 256, P - NEWT),
            "avS": (NEWB, P - NEWT, 256), "bkT": (P, 4 * SEQ), "bkN": (P, 4, NEW), "bv": (TOK, 512),
            "bkS": (NEWB, 512, PAST - NEWT), "bvS": (NEWB, PAST - NEWT, 512)}

    nc = bacc.Bacc("TRN2", target_bir_lowering=False, num_devices=1)
    t = {n: nc.dram_tensor(f"in_{n}", a.shape, F32, kind="ExternalInput").ap() for n, a in feed.items()}
    t |= {n: nc.dram_tensor(f"out_{n}", s, F32, kind="ExternalOutput").ap() for n, s in outs.items()}
    t["u"] = nc.dram_tensor("u", (NG, SEQ, UROW), F32, kind="Internal").ap()
    program(nc, t)
    got = run_bass_kernel_spmd(nc, [{f"in_{n}": a for n, a in feed.items()}], core_ids=[0]).results[0]
    r = {n: np.asarray(got[f"out_{n}"]) for n in outs}

    y = r["yT"].reshape(DM, TOK).T
    ak = r["akT"].transpose(2, 1, 0).reshape(P + NEW, A_KV, HD)
    av = r["avN"].reshape(P + NEW, A_KV, HD)
    bkp = r["bkT"].reshape(P, 4, SEQ).transpose(2, 1, 0).reshape(SEQ, B_SLOTS, HD)
    bkn = r["bkN"].transpose(2, 1, 0).reshape(NEWB, NEWT, B_SLOTS, HD)
    bvp = r["bv"][:SEQ].reshape(SEQ, B_SLOTS, HD)
    bvn = r["bv"][SEQ:].reshape(NEWB, NEWT, B_SLOTS, HD)
    back = np.argsort(ko[NEWT:])
    bks = r["bkS"].transpose(0, 2, 1)[:, back].reshape(NEWB, PAST - NEWT, B_SLOTS, HD)
    bvs = r["bvS"][:, back].reshape(NEWB, PAST - NEWT, B_SLOTS, HD)
    aks = r["akS"].transpose(0, 2, 1).reshape(NEWB, P - NEWT, A_KV, HD)
    avs = r["avS"].reshape(NEWB, P - NEWT, A_KV, HD)
    new = lambda z: z[P:].reshape(NEWB, NEWT, A_KV, HD)
    return (cont(y[:SEQ].reshape(1, SEQ, DM)), cont(y[SEQ:].reshape(NEWB, NEWT, DM)),
            cont(ak[:P][None, None]), cont(av[:P][None, None]), cont(bkp[None]), cont(bvp[None]),
            cont(np.concatenate([aks, new(ak)], 1)[None]), cont(np.concatenate([avs, new(av)], 1)[None]),
            cont(np.concatenate([bks, bkn], 1)), cont(np.concatenate([bvs, bvn], 1)))
```
